# Optimizing a Trainium2 kernel written in Bass

```python
import jax, jax.numpy as jnp
from jax import lax
import numpy as np

D_MODEL = 1024
BATCH = 1
SEQ = 256
DEPTH = 1

HEAD_DIM = 64
ROT_DIM = HEAD_DIM // 4
ROPE_THETA = 500000.0
N_HEADS_A = 8
MOBA_BLOCK = 256
MOBA_TOPK = 3
MOBA_CHUNK = 64
DIL_PAIRS = ((128, 1), (512, 4), (2048, 16))
HEADS_PER_GROUP_B = 4
N_HEADS_B = HEADS_PER_GROUP_B * len(DIL_PAIRS)
WIDTH_A = N_HEADS_A * HEAD_DIM
WIDTH_B = N_HEADS_B * HEAD_DIM
WIDTH_B_OUT = HEADS_PER_GROUP_B * HEAD_DIM
IN_COLS = 3 * WIDTH_A + 3 * WIDTH_B + 2 * D_MODEL
N_EXPERTS = 32
TOP_K = 4
D_FF = D_MODEL
SWIGLU_LIMIT = 7.0
SWIGLU_ALPHA = 1.702
EXPERT_BLOCK = 128
NORM_EPS = 1e-5

kernel_name = "moba_dilated_gated_moe_hybrid"

def rmsnorm(x, g):
    xf = x.astype(jnp.float32)
    y = xf * lax.rsqrt(jnp.mean(xf * xf, axis=-1, keepdims=True) + NORM_EPS)
    return (y * g.astype(jnp.float32)).astype(x.dtype)

def partial_rope(x, pos):
    half = ROT_DIM // 2
    inv = jnp.float32(ROPE_THETA) ** (-jnp.arange(half, dtype=jnp.float32) / half)
    ang = pos.astype(jnp.float32)[:, None] * inv[None, :]
    cos = jnp.cos(ang)[None, :, None, :]
    sin = jnp.sin(ang)[None, :, None, :]
    xr = x[..., :ROT_DIM].astype(jnp.float32)
    x1, x2 = xr[..., :half], xr[..., half:]
    rot = jnp.concatenate([x1 * cos - x2 * sin, x2 * cos + x1 * sin], axis=-1).astype(x.dtype)
    return jnp.concatenate([rot, x[..., ROT_DIM:]], axis=-1)

def attend(s, mask, v, eq):
    s = jnp.where(mask, s, -jnp.inf)
    m = jnp.max(s, axis=-1, keepdims=True)
    m = jnp.where(jnp.isfinite(m), m, 0.0)
    p = jnp.exp(s - m)
    l = jnp.sum(p, axis=-1, keepdims=True)
    o = jnp.einsum(eq, p, v.astype(jnp.float32)) / jnp.maximum(l, 1.0)
    lse = jnp.where(l[..., 0] > 0, m[..., 0] + jnp.log(jnp.maximum(l[..., 0], 1.0)), -jnp.inf)
    return o, lse

def moba_attention(q, k, v):
    B_, S_, H, Dh = q.shape
    nb = -(-S_ // MOBA_BLOCK)
    S_p = nb * MOBA_BLOCK
    pad = ((0, 0), (0, S_p - S_), (0, 0), (0, 0))
    q, k, v = [jnp.pad(t, pad).transpose(0, 2, 1, 3) for t in (q, k, v)]
    scale = HEAD_DIM ** -0.5
    qb = q.reshape(B_, H, nb, MOBA_BLOCK, Dh)
    kb = k.reshape(B_, H, nb, MOBA_BLOCK, Dh)
    vb = v.reshape(B_, H, nb, MOBA_BLOCK, Dh)
    s_own = jnp.einsum('bhnqd,bhnkd->bhnqk', qb, kb).astype(jnp.float32) * scale
    causal = jnp.tril(jnp.ones((MOBA_BLOCK, MOBA_BLOCK), dtype=bool))
    o_own, lse_own = attend(s_own, causal, vb, 'bhnqk,bhnkd->bhnqd')
    o_own = o_own.reshape(B_, H, S_p, Dh)
    lse_own = lse_own.reshape(B_, H, S_p)
    k_mean = jnp.mean(kb.astype(jnp.float32), axis=3)
    gate = jnp.einsum('bhsd,bhnd->bhsn', q.astype(jnp.float32), k_mean)
    q_blk = jnp.arange(S_p) // MOBA_BLOCK
    past = jnp.arange(nb)[None, :] < q_blk[:, None]
    gate = jnp.where(past, gate, -jnp.inf)
    k_sel = min(MOBA_TOPK, nb)
    g_val, g_idx = lax.top_k(gate, k_sel)
    g_ok = jnp.isfinite(g_val)
    nc = S_p // MOBA_CHUNK

    def to_chunks(t):
        return jnp.moveaxis(t.reshape(B_, H, nc, MOBA_CHUNK, *t.shape[3:]), 2, 0)

    gather_blocks = jax.vmap(jax.vmap(lambda blocks, idx: blocks[idx]))

    def past_chunk(args):
        qc, ic, okc = args
        kg = gather_blocks(kb, ic).reshape(B_, H, MOBA_CHUNK, k_sel * MOBA_BLOCK, Dh)
        vg = gather_blocks(vb, ic).reshape(B_, H, MOBA_CHUNK, k_sel * MOBA_BLOCK, Dh)
        s = jnp.einsum('bhqd,bhqnd->bhqn', qc, kg).astype(jnp.float32) * scale
        mask = jnp.repeat(okc, MOBA_BLOCK, axis=-1)
        return attend(s, mask, vg, 'bhqn,bhqnd->bhqd')

    o_past, lse_past = lax.map(past_chunk, (to_chunks(q), to_chunks(g_idx), to_chunks(g_ok)))
    o_past = jnp.moveaxis(o_past, 0, 2).reshape(B_, H, S_p, Dh)
    lse_past = jnp.moveaxis(lse_past, 0, 2).reshape(B_, H, S_p)
    lse = jnp.logaddexp(lse_own, lse_past)
    o = o_own * jnp.exp(lse_own - lse)[..., None] + o_past * jnp.exp(lse_past - lse)[..., None]
    return o.transpose(0, 2, 1, 3)[:, :S_].reshape(B_, S_, H * Dh).astype(v.dtype)

def dilated_group(q, k, v, window, dilation):
    B_, S_, Hg, Dh = q.shape
    band = window // dilation
    span = dilation * band
    S_p = -(-S_ // span) * span
    L = S_p // dilation
    nb = L // band
    scale = HEAD_DIM ** -0.5

    def to_sub(t):
        t = jnp.pad(t, ((0, 0), (0, S_p - S_), (0, 0), (0, 0)))
        t = t.reshape(B_, L, dilation, Hg, Dh).transpose(0, 2, 3, 1, 4)
        return t.reshape(B_, dilation, Hg, nb, band, Dh)

    def with_prev(t):
        prev = jnp.pad(t, ((0, 0), (0, 0), (0, 0), (1, 0), (0, 0), (0, 0)))[:, :, :, :-1]
        return jnp.concatenate([prev, t], axis=4)

    qs, ks, vs = to_sub(q), to_sub(k), to_sub(v)
    kw, vw = with_prev(ks), with_prev(vs)
    s = jnp.einsum('brhnqd,brhnkd->brhnqk', qs, kw).astype(jnp.float32) * scale
    qi = jnp.arange(band)[:, None]
    kj = jnp.arange(2 * band)[None, :]
    dist = qi + band - kj
    in_band = (dist >= 0) & (dist <= band)
    no_prev = (jnp.arange(nb) == 0)[:, None, None] & (kj < band)[None]
    mask = in_band[None] & ~no_prev
    o, lse = attend(s, mask, vw, 'brhnqk,brhnkd->brhnqd')
    o = o.reshape(B_, dilation, Hg, L, Dh).transpose(0, 3, 1, 2, 4).reshape(B_, S_p, Hg, Dh)[:, :S_]
    lse = lse.reshape(B_, dilation, Hg, L).transpose(0, 3, 1, 2).reshape(B_, S_p, Hg)[:, :S_]
    return o, lse

def dilated_attention(q, k, v):
    B_, S_ = q.shape[:2]
    outs, lses = [], []
    for g, (win, dil) in enumerate(DIL_PAIRS):
        sl = slice(g * HEADS_PER_GROUP_B, (g + 1) * HEADS_PER_GROUP_B)
        o, l = dilated_group(q[:, :, sl], k[:, :, sl], v[:, :, sl], win, dil)
        outs.append(o)
        lses.append(l)
    o = jnp.stack(outs)
    wts = jax.nn.softmax(jnp.stack(lses), axis=0)
    out = jnp.sum(wts[..., None] * o, axis=0)
    return out.reshape(B_, S_, WIDTH_B_OUT).astype(v.dtype)

def moe_ffn(h, w_router, b_router, w_gate, b_gate, w_up, b_up, w_down, b_down):
    B_, S_, D = h.shape
    T = B_ * S_
    xt = h.reshape(T, D)
    logits = (xt @ w_router).astype(jnp.float32) + b_router.astype(jnp.float32)
    top_val, top_idx = lax.top_k(logits, TOP_K)
    probs = jax.nn.softmax(top_val, axis=-1)
    n_assign = T * TOP_K
    flat_e = top_idx.reshape(-1)
    flat_tok = jnp.repeat(jnp.arange(T, dtype=jnp.int32), TOP_K)
    flat_p = probs.reshape(-1)
    order = jnp.argsort(flat_e)
    e_sorted = flat_e[order]
    counts = jnp.bincount(flat_e, length=N_EXPERTS)
    padded = (counts + EXPERT_BLOCK - 1) // EXPERT_BLOCK * EXPERT_BLOCK
    start = jnp.cumsum(counts) - counts
    pend = jnp.cumsum(padded)
    pstart = pend - padded
    dest = pstart[e_sorted] + (jnp.arange(n_assign) - start[e_sorted])
    n_rows = -(-n_assign // EXPERT_BLOCK) * EXPERT_BLOCK + N_EXPERTS * EXPERT_BLOCK
    row_tok = jnp.zeros((n_rows,), jnp.int32).at[dest].set(flat_tok[order])
    row_p = jnp.zeros((n_rows,), jnp.float32).at[dest].set(flat_p[order])
    n_blk = n_rows // EXPERT_BLOCK
    blk_expert = jnp.minimum(jnp.searchsorted(pend, jnp.arange(n_blk) * EXPERT_BLOCK, side='right'),
                             N_EXPERTS - 1)
    x_rows = xt[row_tok].reshape(n_blk, EXPERT_BLOCK, D)

    def expert_block(args):
        xb, e = args
        g = xb @ w_gate[e] + b_gate[e]
        u = xb @ w_up[e] + b_up[e]
        g = jnp.minimum(g, SWIGLU_LIMIT)
        u = jnp.clip(u, -SWIGLU_LIMIT, SWIGLU_LIMIT)
        a = g * jax.nn.sigmoid(SWIGLU_ALPHA * g) * (u + 1.0)
        return a @ w_down[e] + b_down[e]

    y_rows = lax.map(expert_block, (x_rows, blk_expert)).reshape(n_rows, D)
    y = jax.ops.segment_sum(y_rows * row_p[:, None].astype(y_rows.dtype), row_tok, num_segments=T)
    return y.reshape(B_, S_, D).astype(h.dtype)

def setup_inputs(seed: int = 0) -> dict:
    key = jax.random.key(seed)
    ks = jax.random.split(key, 20)
    f32 = jnp.float32
    nrm = lambda k, shape, s: jax.random.normal(k, shape, f32) * s
    L, D, E, F = DEPTH, D_MODEL, N_EXPERTS, D_FF
    return {
        "x": nrm(ks[0], (BATCH, SEQ, D), 1.0),
        "ln_mix_g": 1.0 + nrm(ks[1], (L, D), 0.02),
        "w_in": nrm(ks[2], (L, D, IN_COLS), D ** -0.5),
        "b_gate_a": nrm(ks[3], (L, D), 0.02),
        "b_gate_b": nrm(ks[4], (L, D), 0.02),
        "w_o_a": nrm(ks[5], (L, WIDTH_A, D), WIDTH_A ** -0.5),
        "w_o_b": nrm(ks[6], (L, WIDTH_B_OUT, D), WIDTH_B_OUT ** -0.5),
        "w_out": nrm(ks[7], (L, D, D), D ** -0.5),
        "ln_ffn_g": 1.0 + nrm(ks[8], (L, D), 0.02),
        "w_router": nrm(ks[9], (L, D, E), D ** -0.5),
        "b_router": nrm(ks[10], (L, E), 0.01),
        "w_gate": nrm(ks[11], (L, E, D, F), D ** -0.5),
        "b_gate": nrm(ks[12], (L, E, F), 0.01),
        "w_up": nrm(ks[13], (L, E, D, F), D ** -0.5),
        "b_up": nrm(ks[14], (L, E, F), 0.01),
        "w_down": nrm(ks[15], (L, E, F, D), F ** -0.5),
        "b_down": nrm(ks[16], (L, E, D), 0.01),
        "ln_final_g": 1.0 + nrm(ks[17], (D,), 0.02),
    }

def reference(x, ln_mix_g, w_in, b_gate_a, b_gate_b, w_o_a, w_o_b, w_out, ln_ffn_g,
              w_router, b_router, w_gate, b_gate, w_up, b_up, w_down, b_down, ln_final_g):
    B_, S_, _ = x.shape
    pos = jnp.arange(S_)
    splits = [WIDTH_A, 2 * WIDTH_A, 3 * WIDTH_A,
              3 * WIDTH_A + WIDTH_B, 3 * WIDTH_A + 2 * WIDTH_B, 3 * WIDTH_A + 3 * WIDTH_B,
              3 * WIDTH_A + 3 * WIDTH_B + D_MODEL]
    for l in range(DEPTH):
        h = rmsnorm(x, ln_mix_g[l])
        proj = h @ w_in[l]
        qa, ka, va, qb, kb, vb, ga, gb = jnp.split(proj, splits, axis=-1)
        heads = lambda t, n: t.reshape(B_, S_, n, HEAD_DIM)
        qa = partial_rope(heads(qa, N_HEADS_A), pos)
        ka = partial_rope(heads(ka, N_HEADS_A), pos)
        qb = partial_rope(heads(qb, N_HEADS_B), pos)
        kb = partial_rope(heads(kb, N_HEADS_B), pos)
        o_a = moba_attention(qa, ka, heads(va, N_HEADS_A))
        o_b = dilated_attention(qb, kb, heads(vb, N_HEADS_B))
        mix = (jax.nn.sigmoid(ga + b_gate_a[l]) * (o_a @ w_o_a[l])
               + jax.nn.sigmoid(gb + b_gate_b[l]) * (o_b @ w_o_b[l]))
        x = x + mix @ w_out[l]
        h = rmsnorm(x, ln_ffn_g[l])
        x = x + moe_ffn(h, w_router[l], b_router[l], w_gate[l], b_gate[l], w_up[l], b_up[l],
                        w_down[l], b_down[l])
    return rmsnorm(x, ln_final_g)


_drawn_inputs = setup_inputs


def setup_inputs(seed=0):
    import zlib

    import numpy as np

    out = dict(_drawn_inputs(seed))
    spreads = {}
    factors = {'b_gate_a': 8.0,
     'b_gate_b': 21.472,
     'b_gate': 23.994,
     'b_up': 34.946,
     'b_down': 22.798,
     'ln_final_g': 23.799,
     'ln_mix_g': 2.675,
     'b_router': 3.093}
    for name, (base, spread) in spreads.items():
        noise = np.random.default_rng([zlib.crc32(name.encode()), seed]).standard_normal(out[name].shape)
        drawn = base * np.exp(spread * noise) if base else spread * noise
        out[name] = __import__('jax').numpy.asarray(drawn.astype(out[name].dtype))
    for name, factor in factors.items():
        out[name] = (out[name] * factor).astype(out[name].dtype)
    return out
```

```python
from contextlib import ExitStack

import concourse.bass as bass
from concourse import mybir

P = 128
D = 1024
KT = D // P
SEQ = 256
NB = SEQ // P
HD = 64
HEADS_A = 8
HEADS_G = 4
DILATIONS = (1, 4, 16)
BAND = 128
NG = len(DILATIONS)
WIDTH_A = HEADS_A * HD
WIDTH_B = NG * HEADS_G * HD
QKV = 3 * WIDTH_A + 3 * WIDTH_B
ROT = 16
SCALE = HD ** -0.5
EPS = 1e-5
E = 32
TOP_K = 4
SLOTS = 64
MAX_OVER = SEQ * TOP_K // (SLOTS + 1)
LIMIT = 7.0
ALPHA = 1.702
FAR = 4096.0
HIDE = -1.0e30

F32 = mybir.dt.float32
I32 = mybir.dt.int32
U32 = mybir.dt.uint32
ALU = mybir.AluOpType
ACT = mybir.ActivationFunctionType
AX = mybir.AxisListType

CHUNK = 512
QK_CHUNKS = {0: 0, 1: 4, 3: 8, 4: 12, 5: 16}
V_CHUNKS = {2: (0, 512), 6: (512, 512), 7: (1024, 256)}
GATE_CHUNK0 = 8
N_CHUNKS = 12
CHUNK_COL = [0, 512, 1024, 1536, 2048, 2560, 3072, 3584, 3840, 4352, 4864, 5376]
QA, KA, QB, KB = 0, 4, 8, 14

C_ID, C_TRI, C_ONE, C_IOTA, C_EID, C_COS, C_SIN = 0, 128, 256, 384, 448, 449, 481
N_CONST = 513
MASK_A = [(0, 128), (128, 256)]
MASK_B = [(384, 384), (768, 768)]
N_MASK = 1536


def shape_constants():
    import numpy as np
    c = np.zeros((P, N_CONST), np.float32)
    row, col = np.arange(P)[:, None], np.arange(P)[None, :]
    c[:, C_ID:C_ID + P] = row == col
    c[:, C_TRI:C_TRI + P] = row < col
    c[:, C_ONE:C_ONE + P] = 1.0
    c[:, C_IOTA:C_IOTA + 64] = np.arange(64)
    c[:, C_EID] = np.arange(P)
    half = ROT // 2
    inv = np.float32(500000.0) ** (-np.arange(half, dtype=np.float32) / np.float32(half))
    for b in range(NB):
        ang = (np.arange(P) + P * b).astype(np.float32)[:, None] * inv.astype(np.float32)[None, :]
        cos, sin = np.cos(ang).astype(np.float32), np.sin(ang).astype(np.float32)
        c[:, C_COS + b * ROT:C_COS + (b + 1) * ROT] = np.concatenate([cos, cos], 1)
        c[:, C_SIN + b * ROT:C_SIN + (b + 1) * ROT] = np.concatenate([-sin, sin], 1)
    m = np.full((P, N_MASK), HIDE, np.float32)
    for b in range(NB):
        keys = P * (b + 1)
        back = (row + P * b) - np.arange(keys)[None, :]
        at = MASK_A[b][0]
        m[:, at:at + keys][back >= 0] = 0.0
        for g, dil in enumerate(DILATIONS):
            at = MASK_B[b][0] + g * keys
            m[:, at:at + keys][(back >= 0) & (back % dil == 0) & (back <= dil * BAND)] = 0.0
    return c, m


def layer(nc, x, ln_mix_g, w_in, b_gate_a, b_gate_b, w_o_a, w_o_b, w_out, ln_ffn_g, w_router, b_router,
          w_gate, b_gate, w_up, b_up, w_down, b_down, ln_final_g, consts, masks, out):
    ctx = ExitStack()

    def sb(name, shape, dt=F32):
        return ctx.enter_context(nc.sbuf_tensor(name, shape, dt))

    def sem(name):
        return ctx.enter_context(nc.semaphore(name))

    with ctx:
        wg = sb("wg", [P, KT, D])
        wu = sb("wu", [P, KT, D])
        wd = sb("wd", [P, KT, D])
        slots = [wu[:, 0:4, :], wu[:, 4:8, :], wd[:, 0:4, :], wd[:, 4:8, :]]
        slots = [s.rearrange("p a f -> p (a f)").rearrange("p (k c) -> p k c", c=CHUNK) for s in slots]
        woa = wu[:, 0:4, :]
        wob = wu[:, 4:6, :]
        wo = wd

        xs = sb("xs", [P, NB, D])
        xn = sb("xn", [P, NB, D])
        h_t = sb("h_t", [P, KT, SEQ])
        v_tok = sb("v_tok", [P, NB, 1280])
        qk_t = sb("qk_t", [P, 20, SEQ])
        mix_t = qk_t[:, 0:8, :]
        gates = sb("gates", [P, 2, KT, SEQ])
        o_t = sb("o_t", [P, 6, SEQ])
        work = sb("work", [P, 4608])
        stage = [work[:, 0:512], work[:, 512:1024]]
        rot_a = work[:, 1024:1152]
        rot_b = work[:, 1152:1280]
        probs = [work[:, 0:768], work[:, 768:1536]]
        masked = [work[:, 1536:2304], work[:, 2304:3072]]
        p_t = [work[:, 3072:3840], work[:, 3840:4608]]
        cst = sb("cst", [P, N_CONST])
        msk = sb("msk", [P, N_MASK])
        rows = sb("rows", [32, P])
        cols = sb("cols", [P, 32])
        bias_rows = sb("bias_rows", [P, 4, P])
        bias_cols = sb("bias_cols", [P, 2, E * KT])
        b_dn = v_tok[0:E, 0, 0:D]
        w_rt = sb("w_rt", [P, KT, E])
        b_rt = sb("b_rt", [P, E])
        g_fin = msk[:, 0:D]
        stat = sb("stat", [P, 64])
        x_g = gates[:, 0, 0:2, :].rearrange("p a t -> p (a t)").rearrange("p (k c) -> p k c", c=SLOTS)
        g_act = gates[:, 0, 2:4, :].rearrange("p a t -> p (a t)").rearrange("p (k c) -> p k c", c=SLOTS)
        sig = gates[:, 0, 4:6, :].rearrange("p a t -> p (a t)").rearrange("p (k c) -> p k c", c=SLOTS)
        u_act = gates[:, 0, 6:8, :].rearrange("p a t -> p (a t)").rearrange("p (k c) -> p k c", c=SLOTS)
        a_t = gates[:, 1, 0:2, :].rearrange("p a t -> p (a t)").rearrange("p (k c) -> p k c", c=SLOTS)
        y_t = gates[:, 1, 2:4, :].rearrange("p a t -> p (a t)").rearrange("p (k c) -> p k c", c=SLOTS)
        y_rows = gates[0:SLOTS, 1, 4:8, :].rearrange("p a t -> p (a t)")
        sel_t = o_t[0:SLOTS, 0, :]
        sel = work[:, 0:128].rearrange("p (b c) -> p b c", c=SLOTS)
        sel_p = work[:, 128:256].rearrange("p (b c) -> p b c", c=SLOTS)
        iota_o = work[:, 256:320]
        pick = work[:, 512:640].rearrange("p (k e) -> p k e", e=E)
        pick_p = work[:, 640:768].rearrange("p (k e) -> p k e", e=E)
        logits = work[:, 768:832].rearrange("p (b e) -> p b e", e=E)
        chosen = work[:, 832:896].rearrange("p (b e) -> p b e", e=E)
        prob = work[:, 896:960].rearrange("p (b e) -> p b e", e=E)
        pos = work[:, 960:1024].rearrange("p (b e) -> p b e", e=E)
        prob_t = work[0:E, 1024:1280]
        tab = work[0:E, 1280:1344]
        offs = work[:, 1344:1360]
        top_v = work[:, 1400:1416]
        top_f = work[:, 1416:1424]
        top_e = work[:, 1424:1432]
        top_i = sb("top_i", [P, NB, 8], U32)
        over_i = sb("over_i", [1, 20], I32)

        ps = ctx.enter_context(nc.psum_tensor("ps", [P, 8, 512], F32))
        G, U, X, DN, Y = 0, 1, 2, 3, 4

        ident = cst[:, C_ID:C_ID + P]
        tri = cst[:, C_TRI:C_TRI + P]
        ones = cst[:, C_ONE:C_ONE + P]
        iota = cst[:, C_IOTA:C_IOTA + 64]

        ld_x = [sem(f"ld_x{b}") for b in range(NB)]
        ld_cst, ld_msk, ld_rows, ld_small = sem("ld_cst"), sem("ld_msk"), sem("ld_rows"), sem("ld_small")
        ld_chunk = [sem(f"ld_chunk{s}") for s in range(4)]
        ld_wo, ld_wout, ld_gfin, ld_bdn = sem("ld_wo"), sem("ld_wout"), sem("ld_gfin"), sem("ld_bdn")
        ld_piece = [sem(f"ld_piece{j}") for j in range(12)]
        oproj_done, wout_done = sem("oproj_done"), sem("wout_done")
        sq_done, var_ready, rstd_ready, xn_ready = sem("sq_done"), sem("var_ready"), sem("rstd_ready"), sem("xn_ready")
        neg_half = sem("neg_half")
        rows_turned, cols_ready = sem("rows_turned"), sem("cols_ready")
        x_turned, h_ready = sem("x_turned"), sem("h_ready")
        proj_done, proj_read = sem("proj_done"), sem("proj_read")
        rot_step, rotated = sem("rot_step"), sem("rotated")
        qk_turned, qk_ready = sem("qk_turned"), sem("qk_ready")
        scored, soft_step, row_max, exp_done, probs_ready = sem("scored"), sem("soft_step"), sem("row_max"), sem("exp_done"), sem("probs_ready")
        p_turned, p_ready = sem("p_turned"), sem("p_ready")
        pv_done, o_ready = sem("pv_done"), sem("o_ready")
        gate_done, gate_read = sem("gate_done"), sem("gate_read")
        gates_ready = sem("gates_ready")
        mix_step, mix_ready = sem("mix_step"), sem("mix_ready")
        res_ready = sem("res_ready")
        bias_turned, bias_ready = sem("bias_turned"), sem("bias_ready")
        logit_done, rt_step = sem("logit_done"), sem("rt_step")
        rt_exp_in, rt_exp = sem("rt_exp_in"), sem("rt_exp")
        chosen_ready, prob_ready = sem("chosen_ready"), sem("prob_ready")
        pos_done, prob_turned, prob_t_ready = sem("pos_done"), sem("prob_turned"), sem("prob_t_ready")
        count_done, nov_ready, ostart_done, tab_ready, tab_done, over_ready = (
            sem("count_done"), sem("nov_ready"), sem("ostart_done"), sem("tab_ready"), sem("tab_done"), sem("over_ready"))
        pieces_used = sem("pieces_used")
        sel_ready, gathered, xg_ready = sem("sel_ready"), sem("gathered"), sem("xg_ready")
        g_ready, sig_done, act_ready = sem("g_ready"), sem("sig_done"), sem("act_ready")
        dve_step, selp_step = sem("dve_step"), sem("selp_step")
        y_ready = sem("y_ready")
        selp_ready, sel_turned, sel_t_ready = sem("selp_ready"), sem("sel_turned"), sem("sel_t_ready")
        y_turned, y_rows_ready = sem("y_turned"), sem("y_rows_ready")
        combined = sem("combined")
        fin_step, fin_ready, stored = sem("fin_step"), sem("fin_ready"), sem("stored")

        x_v = x[0].rearrange("(b p) d -> b p d", p=P)
        out_v = out[0].rearrange("(b p) d -> b p d", p=P)
        win_v = w_in[0].rearrange("(k p) n -> p k n", p=P)
        row_v = [t[0].rearrange("(k p) -> k p", p=P) for t in (ln_mix_g, b_gate_a, b_gate_b, ln_ffn_g)]
        expert_v = [t[0].rearrange("e (k p) f -> e p k f", p=P) for t in (w_gate, w_up, w_down)]
        bias_v = [t[0].rearrange("(h e) (m p) -> h (e m) p", h=2, p=P) for t in (b_gate, b_up)]
        expert_sb = [wg, wu, wd]

        units = [("a", h, None) for h in range(HEADS_A)]
        units += [("b", j, b) for j in range(HEADS_G) for b in range(NB)]
        N_UNITS = len(units)

        def unit_rows(u):
            kind, h, b = units[u]
            if kind == "a":
                return [(0, 0, 128, MASK_A[0][0]), (1, 128, 256, MASK_A[1][0])]
            return [(b, 0, MASK_B[b][1], MASK_B[b][0])]

        def unit_blocks(u):
            kind, h, b = units[u]
            if kind == "a":
                return [(0, 0, 0, HD * h, True, True), (1, 128, 0, HD * h, True, False),
                        (1, 256, 1, HD * h, False, True)]
            last = NG * (b + 1) - 1
            return [(b, P * (g * (b + 1) + kb), kb, WIDTH_A + HD * (HEADS_G * g + h),
                     g == 0 and kb == 0, g * (b + 1) + kb == last) for g in range(NG) for kb in range(b + 1)]

        def unit_out(u):
            kind, h, b = units[u]
            return (h // 2 if kind == "a" else 4 + h // 2), h % 2

        def width(u):
            return len(unit_blocks(u)) * P

        n_soft = [sum(len(unit_rows(v)) for v in range(u)) for u in range(N_UNITS + 1)]
        closes = [(units[u][1] % 2 == 1 and units[u][2] in (None, 1)) for u in range(N_UNITS)]
        tile_end = [u for u in range(N_UNITS) if closes[u]]

        block = ctx.enter_context(nc.Block())

        @block.sync
        def _(sp):
            for b in range(NB):
                sp.dma_start(xs[:, b, :], x_v[b]).then_inc(ld_x[b], 16)

            def chunk(c):
                if c >= 4:
                    sp.wait_ge(proj_done, NB * (c - 3))
                n = V_CHUNKS[c][1] if c in V_CHUNKS else CHUNK
                sp.dma_start(slots[c % 4][:, :, 0:n], win_v[:, :, CHUNK_COL[c]:CHUNK_COL[c] + n])\
                  .then_inc(ld_chunk[c % 4], 16)

            def piece(m, j, e, s):
                sp.dma_start(expert_sb[m][:, 2 * j:2 * j + 2, :], expert_v[m][e, :, 2 * j:2 * j + 2, :])\
                  .then_inc(s, 16)

            for c in range(5):
                chunk(c)
            sp.dma_start(msk[:], masks).then_inc(ld_msk, 16)
            for c in range(5, N_CHUNKS):
                if c < 9:
                    piece(0, c - 5, 0, ld_piece[c - 5])
                chunk(c)
            sp.wait_ge(gate_done, 8)
            sp.dma_start(woa, w_o_a[0].rearrange("(k p) n -> p k n", p=P)).then_inc(ld_wo, 16)
            sp.dma_start(wob, w_o_b[0].rearrange("(k p) n -> p k n", p=P)).then_inc(ld_wo, 16)
            sp.wait_ge(gate_done, 16)
            sp.dma_start(wo[:], w_out[0].rearrange("(k p) n -> p k n", p=P)).then_inc(ld_wout, 16)
            sp.wait_ge(oproj_done, 8)
            for j in range(4):
                piece(1, j, 0, ld_piece[4 + j])
            sp.dma_start(b_dn, b_down[0]).then_inc(ld_bdn, 16)
            sp.wait_ge(wout_done, 4)
            for j in range(4):
                piece(2, j, 0, ld_piece[8 + j])

            sp.dma_start(g_fin, ln_final_g.rearrange("(a d) -> a d", a=1).broadcast_to([P, D])).then_inc(ld_gfin, 16)

            def item_loads(n, e):
                for q in range(12):
                    sp.wait_ge(pieces_used, 12 * n - 11 + q)
                    piece(q // 4, q % 4, e, ld_piece[q])

            with sp.Fori(1, E) as i:
                item_loads(i, i)
            sp.wait_ge(over_ready, 1)
            count = sp.value_load(over_i[0:1, 16:17], min_val=0, max_val=MAX_OVER)
            with sp.If(count > 0):
                with sp.Fori(0, count) as k:
                    e = sp.value_load(over_i[0:1, bass.ds(k, 1)], min_val=0, max_val=E - 1)
                    item_loads(k + E, e)
            for b in range(NB):
                sp.wait_ge(fin_ready, b + 1)
                sp.dma_start(out_v[b], xn[:, b, :]).then_inc(stored, 16)
            sp.wait_ge(stored, 16 * NB)

        @block.gpsimd
        def _(pool):
            pool.memset(stat[:, 60:62], -0.5).then_inc(neg_half, 1)
            pool.wait_ge(neg_half, 1)
            for n in range(3 * NB):
                pool.wait_ge(var_ready, n + 1)
                pool.tensor_tensor(stat[:, 12 + n:13 + n], stat[:, 6 + n:7 + n], stat[:, 60:61], ALU.pow)\
                    .then_inc(rstd_ready, 1)

        @block.scalar
        def _(act):
            act.dma_start(cst[:], consts).then_inc(ld_cst, 16)
            for r in range(4):
                act.dma_start(rows[8 * r:8 * r + 8, :], row_v[r]).then_inc(ld_rows, 16)
            for m in range(2):
                for h in range(2):
                    act.dma_start(bias_rows[:, 2 * m + h, :], bias_v[m][h]).then_inc(ld_small, 16)
            act.dma_start(w_rt[:], w_router[0].rearrange("(k p) e -> p k e", p=P)).then_inc(ld_small, 16)
            act.dma_start(b_rt[:], b_router.broadcast_to([P, E])).then_inc(ld_small, 16)

            for b in range(NB):
                act.wait_ge(ld_x[b], 16)
                act.activation(h_t[:, 4 * b:4 * b + 4, :].rearrange("p k t -> p (k t)"), xs[:, b, :], ACT.Square,
                               accum_out=stat[:, b:b + 1]).then_inc(sq_done, 1)

            qk_seen = 0
            for c in range(8):
                for b in range(NB):
                    act.wait_ge(proj_done, NB * c + b + 1)
                    if c in QK_CHUNKS:
                        if qk_seen >= 2:
                            act.wait_ge(qk_turned, qk_seen - 1)
                        act.activation(stage[b], ps[:, b, :], ACT.Copy).then_inc(proj_read, 1)
                        qk_seen += 1
                    else:
                        at, n = V_CHUNKS[c]
                        act.activation(v_tok[:, b, at:at + n], ps[:, b, 0:n], ACT.Copy).then_inc(proj_read, 1)

            def evac_gate(t):
                act.wait_ge(gate_done, t + 1)
                act.activation(gates[:, t // 8, t % 8, :], ps[:, t % 2, 0:SEQ], ACT.Identity,
                               bias=cols[:, 8 + t:9 + t]).then_inc(gate_read, 1)

            def exps(u):
                for n, (b, at, w, _m) in enumerate(unit_rows(u)):
                    s = n_soft[u] + n
                    act.wait_ge(row_max, s + 1)
                    act.activation(probs[u % 2][:, at:at + w], masked[u % 2][:, at:at + w], ACT.Exp,
                                   bias=stat[:, 20 + (s % 4):21 + (s % 4)], scale=SCALE,
                                   accum_out=stat[:, 24 + (s % 4):25 + (s % 4)]).then_inc(exp_done, 1)

            def evac_o(t):
                act.wait_ge(pv_done, tile_end[t] + 1)
                act.activation(o_t[:, t, :], ps[:, 6 + t % 2, 0:SEQ], ACT.Copy).then_inc(o_ready, 1)

            act.wait_ge(cols_ready, 1)
            tiles_out = 0
            for u in range(N_UNITS):
                if u >= 2:
                    act.wait_ge(p_turned, u - 1)
                exps(u)
                evac_gate(u)
                while tiles_out < len(tile_end) and tile_end[tiles_out] <= u - 2:
                    evac_o(tiles_out)
                    tiles_out += 1
            while tiles_out < len(tile_end):
                evac_o(tiles_out)
                tiles_out += 1
            act.wait_ge(gate_read, 16)
            for g in range(2):
                v = gates[:, g, :, :].rearrange("p k t -> p (k t)")
                act.activation(v, v, ACT.Sigmoid).then_inc(gates_ready, 1)

            for b in range(NB):
                act.wait_ge(rt_exp_in, b + 1)
                act.activation(top_e[:, 4 * b:4 * b + 4], top_v[:, 8 * b:8 * b + 4], ACT.Exp,
                               bias=stat[:, 30 + b:31 + b], accum_out=stat[:, 32 + b:33 + b]).then_inc(rt_exp, 1)
            act.wait_ge(prob_turned, 1)
            act.activation(prob_t, ps[0:E, DN, 0:SEQ], ACT.Copy).then_inc(prob_t_ready, 1)

            def item_sigmoid(n):
                act.wait_ge(g_ready, n + 1)
                act.activation(sig, g_act, ACT.Sigmoid, scale=ALPHA).then_inc(sig_done, 1)

            def item_rows(n):
                act.wait_ge(sel_turned, n + 1)
                act.activation(sel_t, ps[0:SLOTS, X, 0:SEQ], ACT.Copy).then_inc(sel_t_ready, 1)
                for h, bank in enumerate((G, DN)):
                    act.wait_ge(y_turned, 2 * n + h + 1)
                    act.activation(y_rows[:, 512 * h:512 * h + 512], ps[0:SLOTS, bank, :], ACT.Copy)\
                       .then_inc(y_rows_ready, 1)

            def item_out(n):
                act.wait_ge(pieces_used, 12 * n + 12)
                act.activation(y_t, ps[:, DN, :].rearrange("p (k c) -> p k c", c=SLOTS), ACT.Copy)\
                   .then_inc(y_ready, 1)

            item_sigmoid(0)
            item_out(0)
            with act.Fori(1, E) as i:
                item_sigmoid(i)
                item_rows(i - 1)
                item_out(i)
            item_rows(E - 1)
            act.wait_ge(over_ready, 1)
            count = act.value_load(over_i[0:1, 16:17], min_val=0, max_val=MAX_OVER)
            with act.If(count > 0):
                with act.Fori(0, count) as k:
                    item_sigmoid(k + E)
                    item_out(k + E)
                    item_rows(k + E)

        @block.tensor
        def _(pe):
            def turn(out_ap, in_ap):
                n = in_ap.shape[0]
                return pe.transpose(out_ap, in_ap, ident[0:n, 0:n])

            pe.wait_ge(ld_cst, 16)
            pe.wait_ge(ld_rows, 64)
            turn(ps[:, 6, 0:32], rows[:]).then_inc(rows_turned, 1)
            for b in range(NB):
                pe.wait_ge(xn_ready, b + 1)
                for h in range(2):
                    for k in range(4):
                        mm = turn(ps[:, 2 + 2 * b + h, P * k:P * k + P], xn[:, b, P * (4 * h + k):P * (4 * h + k) + P])
                    mm.then_inc(x_turned, 1)
            pe.wait_ge(ld_small, 16 * 6)
            for m in range(2):
                for h in range(2):
                    mm = turn(ps[:, 7, P * (2 * m + h):P * (2 * m + h) + P], bias_rows[:, 2 * m + h, :])
            mm.then_inc(bias_turned, 1)

            qk_turns = 0

            def turn_qk(c):
                nonlocal qk_turns
                for b in range(NB):
                    pe.wait_ge(rotated, qk_turns + 1)
                    if qk_turns >= 2:
                        pe.wait_ge(qk_ready, qk_turns - 1)
                    for k in range(4):
                        mm = turn(ps[:, 2 + b, P * k:P * k + P], stage[b][:, P * k:P * k + P])
                    mm.then_inc(qk_turned, 1)
                    qk_turns += 1

            for c in range(8):
                pe.wait_ge(ld_chunk[c % 4], 16 * (c // 4 + 1))
                n = V_CHUNKS[c][1] if c in V_CHUNKS else CHUNK
                for b in range(NB):
                    if c == 0:
                        pe.wait_ge(h_ready, 2 * (b + 1))
                    else:
                        pe.wait_ge(proj_read, NB * (c - 1) + b + 1)
                    for k in range(KT):
                        mm = pe.matmul(ps[:, b, 0:n], h_t[:, k, P * b:P * b + P], slots[c % 4][:, k, 0:n],
                                       start=(k == 0), stop=(k == KT - 1))
                    mm.then_inc(proj_done, 1)
                if c >= 1 and (c - 1) in QK_CHUNKS:
                    turn_qk(c - 1)

            def scores(u):
                kind, h, b = units[u]
                base = 2 + 2 * (u % 2)
                if u >= 2:
                    pe.wait_ge(p_ready, u - 1)
                if kind == "a":
                    r = HD * (h % 2)
                    q, k = qk_t[r:r + HD, QA + h // 2, :], qk_t[r:r + HD, KA + h // 2, :]
                    pe.matmul(ps[:, base, 0:128], q[:, 0:128], k[:, 0:128], start=True, stop=True)
                    mm = pe.matmul(ps[:, base, 128:384], q[:, 128:256], k[:, 0:256], start=True, stop=True)
                else:
                    keys = P * (b + 1)
                    for g in range(NG):
                        hh = HEADS_G * g + h
                        r = HD * (hh % 2)
                        q, k = qk_t[r:r + HD, QB + hh // 2, :], qk_t[r:r + HD, KB + hh // 2, :]
                        at = g * keys
                        mm = pe.matmul(ps[:, base + at // 512, at % 512:at % 512 + keys], q[:, P * b:P * b + P],
                                       k[:, 0:keys], start=True, stop=True)
                mm.then_inc(scored, 1)

            def gate_tile(t):
                c = GATE_CHUNK0 + t // 4
                if t % 4 == 0:
                    pe.wait_ge(ld_chunk[c % 4], 16 * (c // 4 + 1))
                if t >= 2:
                    pe.wait_ge(gate_read, t - 1)
                else:
                    pe.wait_ge(proj_read, 16)
                for k in range(KT):
                    mm = pe.matmul(ps[:, t % 2, 0:SEQ], slots[c % 4][:, k, P * (t % 4):P * (t % 4) + P],
                                   h_t[:, k, :], start=(k == 0), stop=(k == KT - 1))
                mm.then_inc(gate_done, 1)

            def turn_probs(u):
                base = 2 + 2 * (u % 2)
                pe.wait_ge(probs_ready, n_soft[u + 1])
                for (_b, at, _k, _v, _f, _l) in unit_blocks(u):
                    mm = turn(ps[:, base + at // 512, at % 512:at % 512 + P], probs[u % 2][:, at:at + P])
                mm.then_inc(p_turned, 1)

            def weigh_values(u):
                t, half = unit_out(u)
                pe.wait_ge(p_ready, u + 1)
                if t >= 2:
                    pe.wait_ge(o_ready, t - 1)
                for (b, at, kb, v, first, last) in unit_blocks(u):
                    mm = pe.matmul(ps[HD * half:HD * half + HD, 6 + t % 2, P * b:P * b + P],
                                   v_tok[:, kb, v:v + HD], p_t[u % 2][:, at:at + P], start=first, stop=last)
                mm.then_inc(pv_done, 1)

            pe.wait_ge(qk_ready, 10)
            pe.wait_ge(bias_ready, 1)
            scores(0)
            for u in range(N_UNITS):
                gate_tile(u)
                if u + 1 < N_UNITS:
                    scores(u + 1)
                turn_probs(u)
                if u >= 1:
                    weigh_values(u - 1)
            weigh_values(N_UNITS - 1)

            pe.wait_ge(ld_wo, 32)
            pe.wait_ge(o_ready, 6)
            for m in range(KT):
                if m < 2:
                    pe.wait_ge(gate_read, 15 + m)
                else:
                    pe.wait_ge(mix_ready, m - 1)
                for k in range(4):
                    pe.matmul(ps[:, m % 2, 0:SEQ], woa[:, k, P * m:P * m + P], o_t[:, k, :],
                              start=(k == 0), stop=(k == 3))
                for k in range(2):
                    mm = pe.matmul(ps[:, m % 2, SEQ:2 * SEQ], wob[:, k, P * m:P * m + P], o_t[:, 4 + k, :],
                                   start=(k == 0), stop=(k == 1))
                mm.then_inc(oproj_done, 1)
            pe.wait_ge(ld_wout, 16)
            for b in range(NB):
                for h in range(2):
                    for k in range(KT):
                        pe.wait_ge(mix_ready, k + 1) if b == 0 and h == 0 else None
                        mm = pe.matmul(ps[:, 2 + 2 * b + h, :], mix_t[:, k, P * b:P * b + P],
                                       wo[:, k, 512 * h:512 * h + 512], start=(k == 0), stop=(k == KT - 1))
                    mm.then_inc(wout_done, 1)

            for b in range(NB):
                pe.wait_ge(xn_ready, NB + b + 1)
                for h in range(2):
                    if b == 1:
                        pe.wait_ge(h_ready, 4 + h + 1)
                    for k in range(4):
                        mm = turn(ps[:, 6 + h, P * k:P * k + P], xn[:, b, P * (4 * h + k):P * (4 * h + k) + P])
                    mm.then_inc(x_turned, 1)
                pe.wait_ge(h_ready, 4 + 2 * b + 2)
                for k in range(KT):
                    mm = pe.matmul(ps[:, b, 0:E], h_t[:, k, P * b:P * b + P], w_rt[:, k, :],
                                   start=(k == 0), stop=(k == KT - 1))
                mm.then_inc(logit_done, 1)
            pe.wait_ge(chosen_ready, 2)
            pe.matmul(ps[:, U, 0:E], tri, chosen[:, 0, :], start=True, stop=True)
            pe.matmul(ps[:, U, E:2 * E], ones, chosen[:, 0, :], start=True, stop=False)
            pe.matmul(ps[:, U, E:2 * E], tri, chosen[:, 1, :], start=False, stop=True).then_inc(pos_done, 1)
            for b in range(NB):
                mm = pe.matmul(ps[0:E, G, 0:1], chosen[:, b, :], ones[:, 0:1], start=(b == 0), stop=(b == NB - 1))
            mm.then_inc(count_done, 1)
            pe.wait_ge(prob_ready, 2)
            for b in range(NB):
                mm = turn(ps[0:E, DN, P * b:P * b + P], prob[:, b, :])
            mm.then_inc(prob_turned, 1)

            def gather(n):
                pe.wait_ge(sel_ready, n + 1)
                for k in range(KT):
                    for b in range(NB):
                        mm = pe.matmul(ps[:, X, SLOTS * k:SLOTS * k + SLOTS], xn[:, b, P * k:P * k + P], sel[:, b, :],
                                       start=(k == 0 and b == 0), stop=(b == NB - 1), skip_group_check=True)
                mm.then_inc(gathered, 1)

            def product(m, n, bank, rhs):
                for j in range(4):
                    pe.wait_ge(ld_piece[4 * m + j], 16 * n + 16)
                    for k in (2 * j, 2 * j + 1):
                        for f in range(KT):
                            mm = pe.matmul(ps[:, bank, SLOTS * f:SLOTS * f + SLOTS],
                                           expert_sb[m][:, k, P * f:P * f + P], rhs[:, k, :],
                                           start=(k == 0 and f == 0), stop=(k == KT - 1), skip_group_check=True)
                    mm.then_inc(pieces_used, 1)

            def turn_item(n, bank_g_read=None):
                pe.wait_ge(ld_cst, 16)
                if bank_g_read is not None:
                    pe.wait_ge(g_ready, bank_g_read)
                pe.wait_ge(selp_ready, n + 1)
                pe.wait_ge(y_ready, n + 1)
                for b in range(NB):
                    mm = turn(ps[0:SLOTS, X, P * b:P * b + P], sel_p[:, b, :])
                mm.then_inc(sel_turned, 1)
                for h, bank in enumerate((G, DN)):
                    for k in range(4):
                        mm = turn(ps[0:SLOTS, bank, P * k:P * k + P], y_t[:, 4 * h + k, :])
                    mm.then_inc(y_turned, 1)

            def combine(n):
                pe.wait_ge(sel_t_ready, n + 1)
                for h in range(2):
                    pe.wait_ge(y_rows_ready, 2 * n + h + 1)
                    for b in range(NB):
                        mm = pe.matmul(ps[:, Y + 2 * b + h, :], sel_t[:, P * b:P * b + P],
                                       y_rows[:, 512 * h:512 * h + 512], start=False, stop=False,
                                       skip_group_check=True)
                mm.then_inc(combined, 1)

            gather(0)
            pe.wait_ge(prob_t_ready, 1)
            pe.wait_ge(ld_bdn, 16)
            pe.wait_ge(res_ready, 4)
            for b in range(NB):
                for h in range(2):
                    pe.matmul(ps[:, Y + 2 * b + h, :], prob_t[:, P * b:P * b + P], b_dn[:, 512 * h:512 * h + 512],
                              start=True, stop=False, skip_group_check=True)
            pe.wait_ge(nov_ready, 1)
            pe.matmul(ps[0:E, DN, 0:1], tri[0:E, 0:E], tab[:, 32:33], start=True, stop=True).then_inc(ostart_done, 1)
            pe.wait_ge(xg_ready, 1)
            product(0, 0, G, x_g)
            pe.wait_ge(tab_ready, 1)
            pe.matmul(ps[:, DN, 0:33], ones[0:E, :], tab[:, 0:33], start=True, stop=True).then_inc(tab_done, 1)
            product(1, 0, U, x_g)
            gather(1)
            pe.wait_ge(over_ready, 1)
            pe.wait_ge(act_ready, 1)
            product(2, 0, DN, a_t)
            with pe.Fori(1, E - 1) as i:
                pe.wait_ge(xg_ready, i + 1)
                product(0, i, G, x_g)
                product(1, i, U, x_g)
                turn_item(i - 1, i + 1)
                pe.wait_ge(sel_t_ready, i)
                gather(i + 1)
                combine(i - 1)
                pe.wait_ge(act_ready, i + 1)
                product(2, i, DN, a_t)
            n = E - 1
            pe.wait_ge(xg_ready, n + 1)
            product(0, n, G, x_g)
            product(1, n, U, x_g)
            turn_item(n - 1, n + 1)
            combine(n - 1)
            pe.wait_ge(act_ready, n + 1)
            product(2, n, DN, a_t)
            turn_item(n)
            combine(n)

            count = pe.value_load(over_i[0:1, 16:17], min_val=0, max_val=MAX_OVER)
            with pe.If(count > 0):
                with pe.Fori(0, count) as k:
                    n = k + E
                    gather(n)
                    pe.wait_ge(xg_ready, n + 1)
                    product(0, n, G, x_g)
                    product(1, n, U, x_g)
                    pe.wait_ge(act_ready, n + 1)
                    product(2, n, DN, a_t)
                    turn_item(n)
                    combine(n)

        @block.vector
        def _(dve):
            def variance(n):
                dve.tensor_scalar(stat[:, 6 + n:7 + n], stat[:, n:n + 1], 1.0 / D, EPS, ALU.mult, ALU.add)\
                   .then_inc(var_ready, 1)

            def normalise(n, b):
                dve.wait_ge(rstd_ready, n + 1)
                dve.tensor_scalar(xn[:, b, :], xs[:, b, :], stat[:, 12 + n:13 + n], None, ALU.mult)\
                   .then_inc(xn_ready, 1)

            dve.wait_ge(rows_turned, 1)
            dve.tensor_copy(cols[:], ps[:, 6, 0:32]).then_inc(cols_ready, 1)
            for b in range(NB):
                dve.wait_ge(sq_done, b + 1)
                variance(b)
            for b in range(NB):
                normalise(b, b)
            dve.wait_ge(cols_ready, 1)

            def spread(col, n):
                return col.rearrange("p (k a) -> p k a", a=1).broadcast_to([P, n[0], n[1]])

            for b in range(NB):
                for h in range(2):
                    dve.wait_ge(x_turned, 2 * b + h + 1)
                    if b == 0 and h == 0:
                        dve.wait_ge(sq_done, 2)
                    dve.tensor_tensor(h_t[:, 4 * h:4 * h + 4, P * b:P * b + P],
                                      ps[:, 2 + 2 * b + h, :].rearrange("p (k t) -> p k t", t=P),
                                      spread(cols[:, 4 * h:4 * h + 4], (4, P)), ALU.mult).then_inc(h_ready, 1)
            dve.wait_ge(bias_turned, 1)
            dve.tensor_copy(bias_cols[:].rearrange("p m e -> p (m e)"), ps[:, 7, :]).then_inc(bias_ready, 1)

            steps = 0
            seen = 0
            turned_out = 0

            def qk_out(c):
                nonlocal turned_out
                t0 = QK_CHUNKS[c]
                for b in range(NB):
                    dve.wait_ge(qk_turned, turned_out + 1)
                    dve.tensor_copy(qk_t[:, t0:t0 + 4, P * b:P * b + P],
                                    ps[:, 2 + b, :].rearrange("p (k t) -> p k t", t=P)).then_inc(qk_ready, 1)
                    turned_out += 1

            for c in range(8):
                if c in QK_CHUNKS:
                    for b in range(NB):
                        dve.wait_ge(proj_read, NB * c + b + 1)
                        s = stage[b].rearrange("p (h d) -> p h d", d=HD)
                        ra = rot_a.rearrange("p (h d) -> p h d", d=ROT)
                        rb = rot_b.rearrange("p (h d) -> p h d", d=ROT)
                        cos = cst[:, C_COS + ROT * b:C_COS + ROT * b + ROT].rearrange("p (a d) -> p a d", a=1)
                        sin = cst[:, C_SIN + ROT * b:C_SIN + ROT * b + ROT].rearrange("p (a d) -> p a d", a=1)
                        if steps:
                            dve.wait_ge(rotated, seen)
                        dve.tensor_tensor(ra, s[:, :, 0:ROT], cos.broadcast_to([P, 8, ROT]), ALU.mult).then_inc(rot_step, 1)
                        dve.tensor_tensor(rb[:, :, 0:8], s[:, :, 8:16], sin[:, :, 0:8].broadcast_to([P, 8, 8]), ALU.mult)\
                           .then_inc(rot_step, 1)
                        dve.tensor_tensor(rb[:, :, 8:16], s[:, :, 0:8], sin[:, :, 8:16].broadcast_to([P, 8, 8]), ALU.mult)\
                           .then_inc(rot_step, 1)
                        steps += 3
                        dve.wait_ge(rot_step, steps)
                        dve.tensor_tensor(s[:, :, 0:ROT], ra, rb, ALU.add).then_inc(rotated, 1)
                        seen += 1
                if c >= 1 and (c - 1) in QK_CHUNKS:
                    qk_out(c - 1)

            dve.wait_ge(ld_msk, 16)
            dve.wait_ge(qk_turned, 10)
            soft_steps = 0

            def row_maxima(u):
                nonlocal soft_steps
                base = 2 + 2 * (u % 2)
                flat = ps[:, base:base + 2, :].rearrange("p a c -> p (a c)")
                dve.wait_ge(scored, u + 1)
                if u >= 2:
                    dve.wait_ge(exp_done, n_soft[u - 1])
                for n, (b, at, w, mk) in enumerate(unit_rows(u)):
                    s = n_soft[u] + n
                    dve.tensor_tensor_reduce(masked[u % 2][:, at:at + w], flat[:, at:at + w], msk[:, mk:mk + w],
                                             1.0, HIDE, ALU.add, ALU.max, stat[:, 28 + n:29 + n]).then_inc(soft_step, 1)
                    soft_steps += 1
                    dve.wait_ge(soft_step, soft_steps)
                    if s >= 4:
                        dve.wait_ge(exp_done, s - 3)
                    dve.tensor_scalar(stat[:, 20 + (s % 4):21 + (s % 4)], stat[:, 28 + n:29 + n], -SCALE, None, ALU.mult)\
                       .then_inc(row_max, 1)

            def divide(u):
                nonlocal soft_steps
                for n, (b, at, w, _m) in enumerate(unit_rows(u)):
                    s = n_soft[u] + n
                    dve.wait_ge(exp_done, s + 1)
                    dve.reciprocal(stat[:, 34 + (s % 4):35 + (s % 4)], stat[:, 24 + (s % 4):25 + (s % 4)]).then_inc(soft_step, 1)
                    soft_steps += 1
                    dve.wait_ge(soft_step, soft_steps)
                    pr = probs[u % 2][:, at:at + w]
                    dve.tensor_scalar(pr, pr, stat[:, 34 + (s % 4):35 + (s % 4)], None, ALU.mult).then_inc(probs_ready, 1)

            def probs_out(u):
                base = 2 + 2 * (u % 2)
                w = width(u)
                dve.wait_ge(p_turned, u + 1)
                if u >= 2:
                    dve.wait_ge(pv_done, u - 1)
                dve.tensor_copy(p_t[u % 2][:, 0:w], ps[:, base:base + 2, :].rearrange("p a c -> p (a c)")[:, 0:w])\
                   .then_inc(p_ready, 1)

            row_maxima(0)
            for u in range(N_UNITS):
                divide(u)
                if u + 1 < N_UNITS:
                    row_maxima(u + 1)
                probs_out(u)

            dve.wait_ge(gates_ready, 2)
            for m in range(KT):
                dve.wait_ge(oproj_done, m + 1)
                ta, tb = work[:, 512 * (m % 2):512 * (m % 2) + 256], work[:, 512 * (m % 2) + 256:512 * (m % 2) + 512]
                dve.tensor_tensor(ta, ps[:, m % 2, 0:SEQ], gates[:, 0, m, :], ALU.mult).then_inc(mix_step, 1)
                dve.tensor_tensor(tb, ps[:, m % 2, SEQ:2 * SEQ], gates[:, 1, m, :], ALU.mult).then_inc(mix_step, 1)
                dve.wait_ge(mix_step, 2 * m + 2)
                dve.tensor_tensor(mix_t[:, m, :], ta, tb, ALU.add).then_inc(mix_ready, 1)
            dve.wait_ge(mix_ready, KT)

            for b in range(NB):
                for h in range(2):
                    q = slice(512 * h, 512 * h + 512)
                    dve.wait_ge(wout_done, 2 * b + h + 1)
                    dve.tensor_tensor(xs[:, b, q], xs[:, b, q], ps[:, 2 + 2 * b + h, :], ALU.add).then_inc(res_ready, 1)
                dve.wait_ge(res_ready, 2 * b + 2)
                dve.tensor_tensor_reduce(work[:, 1024:2048], xs[:, b, :], xs[:, b, :], 1.0, 0.0, ALU.mult, ALU.add,
                                         stat[:, 2 + b:3 + b]).then_inc(sq_done, 1)
                dve.wait_ge(sq_done, NB + b + 1)
                variance(NB + b)
                normalise(NB + b, b)

            rt = 0

            def step(ins):
                nonlocal rt
                rt += 1
                ins.then_inc(rt_step, 1)
                dve.wait_ge(rt_step, rt)

            for b in range(NB):
                for h in range(2):
                    dve.wait_ge(x_turned, 4 + 2 * b + h + 1)
                    dve.tensor_tensor(h_t[:, 4 * h:4 * h + 4, P * b:P * b + P],
                                      ps[:, 6 + h, :].rearrange("p (k t) -> p k t", t=P),
                                      spread(cols[:, 24 + 4 * h:24 + 4 * h + 4], (4, P)), ALU.mult).then_inc(h_ready, 1)
            for b in range(NB):
                dve.wait_ge(logit_done, b + 1)
                lg, tv = logits[:, b, :], top_v[:, 8 * b:8 * b + 8]
                step(dve.tensor_tensor(lg, ps[:, b, 0:E], b_rt[:], ALU.add))
                step(dve.max(tv, lg))
                dve.tensor_scalar(stat[:, 30 + b:31 + b], tv[:, 0:1], -1.0, None, ALU.mult).then_inc(rt_exp_in, 1)
                step(dve.max_index(top_i[:, b, :], tv, lg))
                step(dve.tensor_copy(top_f[:, 4 * b:4 * b + 4], top_i[:, b, 0:4]))
                step(dve.tensor_tensor(pick, iota[:, 0:E].rearrange("p (a e) -> p a e", a=1).broadcast_to([P, TOP_K, E]),
                                       spread(top_f[:, 4 * b:4 * b + 4], (TOP_K, E)), ALU.is_equal))
                dve.tensor_reduce(chosen[:, b, :], pick.rearrange("p k e -> p e k"), AX.X, ALU.add).then_inc(chosen_ready, 1)
                dve.wait_ge(rt_exp, b + 1)
                step(dve.reciprocal(stat[:, 40 + b:41 + b], stat[:, 32 + b:33 + b]))
                step(dve.tensor_scalar(top_e[:, 4 * b:4 * b + 4], top_e[:, 4 * b:4 * b + 4], stat[:, 40 + b:41 + b], None, ALU.mult))
                step(dve.tensor_tensor(pick_p, pick, spread(top_e[:, 4 * b:4 * b + 4], (TOP_K, E)), ALU.mult))
                dve.tensor_reduce(prob[:, b, :], pick_p.rearrange("p k e -> p e k"), AX.X, ALU.add).then_inc(prob_ready, 1)
                dve.wait_ge(prob_ready, b + 1)
            dve.wait_ge(chosen_ready, 2)
            step(dve.tensor_scalar(pos, chosen, FAR, -FAR, ALU.mult, ALU.add))
            dve.wait_ge(pos_done, 1)
            step(dve.tensor_tensor(pos, pos, ps[:, U, 0:2 * E].rearrange("p (b e) -> p b e", e=E), ALU.add))

            iota_b = iota.rearrange("p (a c) -> p a c", a=1).broadcast_to([P, NB, SLOTS])

            def at_expert(tab_ap, e):
                return tab_ap[:, :, bass.ds(e, 1)].broadcast_to([P, NB, SLOTS])

            def select(e, slot_ids=iota_b):
                dve.tensor_tensor(sel, slot_ids, at_expert(pos, e), ALU.is_equal).then_inc(sel_ready, 1)

            def select_p(n, e, slot_ids=iota_b):
                dve.tensor_tensor(sel_p, slot_ids, at_expert(pos, e), ALU.is_equal).then_inc(selp_step, 1)
                dve.wait_ge(selp_step, n + 1)
                dve.tensor_tensor(sel_p, sel_p, at_expert(prob, e), ALU.mult).then_inc(selp_ready, 1)

            def slots_of(bank):
                return ps[:, bank, :].rearrange("p (k c) -> p k c", c=SLOTS)

            def bias_of(m, e):
                return bias_cols[:, m, bass.ds(e * KT, KT)].rearrange("p (k a) -> p k a", a=1).broadcast_to([P, KT, SLOTS])

            def gathered_out(n):
                dve.wait_ge(gathered, n + 1)
                dve.tensor_tensor(x_g, slots_of(X), spread(cols[:, 24:32], (KT, SLOTS)), ALU.mult).then_inc(xg_ready, 1)

            def gate_part(n, e):
                dve.wait_ge(pieces_used, 12 * n + 4)
                dve.tensor_tensor(g_act, slots_of(G), bias_of(0, e), ALU.add).then_inc(dve_step, 1)
                dve.wait_ge(dve_step, 4 * n + 1)
                dve.tensor_scalar(g_act, g_act, LIMIT, None, ALU.min).then_inc(g_ready, 1)

            def up_part(n, e):
                dve.wait_ge(pieces_used, 12 * n + 8)
                dve.tensor_tensor(u_act, slots_of(U), bias_of(1, e), ALU.add).then_inc(dve_step, 1)
                dve.wait_ge(dve_step, 4 * n + 2)
                dve.tensor_scalar(u_act, u_act, LIMIT, -LIMIT, ALU.min, ALU.max).then_inc(dve_step, 1)
                dve.wait_ge(sig_done, n + 1)
                dve.tensor_tensor(sig, g_act, sig, ALU.mult).then_inc(dve_step, 1)
                dve.wait_ge(dve_step, 4 * n + 4)
                dve.scalar_tensor_tensor(a_t, u_act, 1.0, sig, ALU.add, ALU.mult).then_inc(act_ready, 1)

            select(0)
            dve.wait_ge(count_done, 1)
            cnt = ps[0:E, G, 0:1]
            step(dve.tensor_scalar(tab[:, 33:34], cnt, float(SLOTS), None, ALU.is_gt))
            step(dve.tensor_scalar(tab[:, 34:35], cnt, float(2 * SLOTS), None, ALU.is_gt))
            step(dve.tensor_scalar(tab[:, 35:36], cnt, float(3 * SLOTS), None, ALU.is_gt))
            dve.tensor_reduce(tab[:, 32:33], tab[:, 33:36], AX.X, ALU.add).then_inc(nov_ready, 1)
            dve.wait_ge(nov_ready, 1)
            gathered_out(0)
            dve.wait_ge(ostart_done, 1)
            step(dve.tensor_scalar(tab[:, 36:52], iota[0:E, 0:16], ps[0:E, DN, 0:1], None, ALU.subtract))
            step(dve.tensor_scalar(tab[:, 0:16], tab[:, 36:52], tab[:, 32:33], None, ALU.is_lt))
            step(dve.tensor_scalar(tab[:, 16:32], tab[:, 36:52], 0.0, None, ALU.is_ge))
            step(dve.tensor_tensor(tab[:, 16:32], tab[:, 0:16], tab[:, 16:32], ALU.mult))
            step(dve.tensor_scalar(tab[:, 36:52], tab[:, 36:52], 1.0, float(SLOTS), ALU.add, ALU.mult))
            step(dve.tensor_tensor(tab[:, 0:16], tab[:, 36:52], tab[:, 16:32], ALU.mult))
            dve.tensor_scalar(tab[:, 16:32], tab[:, 16:32], cst[0:E, C_EID:C_EID + 1], None, ALU.mult).then_inc(tab_ready, 1)
            dve.wait_ge(gathered, 1)
            select(1)
            dve.wait_ge(tab_done, 1)
            step(dve.tensor_copy(offs, ps[:, DN, 0:16]))
            dve.tensor_copy(over_i[0:1, 0:17], ps[0:1, DN, 16:33]).then_inc(over_ready, 1)
            gate_part(0, 0)
            up_part(0, 0)
            gathered_out(1)
            with dve.Fori(1, E - 1) as i:
                select(i + 1)
                select_p(i - 1, i - 1)
                gate_part(i, i)
                up_part(i, i)
                gathered_out(i + 1)
            select_p(E - 2, E - 2)
            gate_part(E - 1, E - 1)
            up_part(E - 1, E - 1)
            dve.wait_ge(sel_turned, E - 1)
            select_p(E - 1, E - 1)

            count = dve.value_load(over_i[0:1, 16:17], min_val=0, max_val=MAX_OVER)
            with dve.If(count > 0):
                with dve.Fori(0, count) as k:
                    n = k + E
                    e = dve.value_load(over_i[0:1, bass.ds(k, 1)], min_val=0, max_val=E - 1)
                    dve.wait_ge(sel_turned, n)
                    dve.tensor_tensor(iota_o, iota, offs[:, bass.ds(k, 1)].broadcast_to([P, SLOTS]), ALU.add)\
                       .then_inc(fin_step, 1)
                    dve.wait_ge(fin_step, k + 1)
                    ids = iota_o.rearrange("p (a c) -> p a c", a=1).broadcast_to([P, NB, SLOTS])
                    select(e, ids)
                    gathered_out(n)
                    select_p(n, e, ids)
                    gate_part(n, e)
                    up_part(n, e)

            dve.wait_ge(combined, count + E)
            dve.wait_ge(ld_gfin, 16)
            for b in range(NB):
                dve.tensor_tensor(xs[:, b, :], xs[:, b, :], ps[:, Y + 2 * b:Y + 2 * b + 2, :].rearrange("p a c -> p (a c)"),
                                  ALU.add).then_inc(res_ready, 1)
                dve.wait_ge(res_ready, 4 + b + 1)
                dve.tensor_tensor_reduce(work[:, 1536:2560], xs[:, b, :], xs[:, b, :], 1.0, 0.0, ALU.mult, ALU.add,
                                         stat[:, 4 + b:5 + b]).then_inc(sq_done, 1)
                dve.wait_ge(sq_done, 2 * NB + b + 1)
                variance(2 * NB + b)
            for b in range(NB):
                normalise(2 * NB + b, b)
                dve.wait_ge(xn_ready, 2 * NB + b + 1)
                dve.tensor_tensor(xn[:, b, :], xn[:, b, :], g_fin[:], ALU.mult).then_inc(fin_ready, 1)


_INS = ["x", "ln_mix_g", "w_in", "b_gate_a", "b_gate_b", "w_o_a", "w_o_b", "w_out", "ln_ffn_g", "w_router", "b_router",
        "w_gate", "b_gate", "w_up", "b_up", "w_down", "b_down", "ln_final_g"]


def kernel(**inputs):
    import numpy as _np
    import concourse.bacc as _bacc
    from concourse import mybir as _mybir
    from concourse.bass_utils import run_bass_kernel_spmd as _run

    nc = _bacc.Bacc("TRN2", target_bir_lowering=False, num_devices=1)
    arrays, args = {}, []
    given = {name: _np.ascontiguousarray(inputs[name]) for name in _INS}
    given["consts"], given["masks"] = shape_constants()
    for name, a in given.items():
        arrays[f"in_{name}_dram"] = a
        args.append(nc.dram_tensor(f"in_{name}_dram", a.shape, _mybir.dt.from_np(a.dtype), kind="ExternalInput").ap())
    out = nc.dram_tensor("out_dram", (1, SEQ, D), _mybir.dt.float32, kind="ExternalOutput").ap()
    layer(nc, *args, out)
    r = _run(nc, [arrays], core_ids=[0])
    return r.results[0]["out_dram"]
```

```python
from contextlib import ExitStack

import concourse.bass as bass
from concourse import mybir

P = 128
D = 1024
KT = D // P
SEQ = 256
NB = SEQ // P
HD = 64
HEADS_A = 8
HEADS_G = 4
DILATIONS = (1, 4, 16)
BAND = 128
NG = len(DILATIONS)
WIDTH_A = HEADS_A * HD
WIDTH_B = NG * HEADS_G * HD
QKV = 3 * WIDTH_A + 3 * WIDTH_B
ROT = 16
SCALE = HD ** -0.5
EPS = 1e-5
E = 32
TOP_K = 4
SLOTS = 64
MAX_OVER = SEQ * TOP_K // (SLOTS + 1)
LIMIT = 7.0
ALPHA = 1.702
FAR = 4096.0
HIDE = -1.0e30

F32 = mybir.dt.float32
I32 = mybir.dt.int32
U32 = mybir.dt.uint32
ALU = mybir.AluOpType
ACT = mybir.ActivationFunctionType
AX = mybir.AxisListType

CHUNK = 512
QK_CHUNKS = {0: 0, 1: 4, 3: 8, 4: 12, 5: 16}
V_CHUNKS = {2: (0, 512), 6: (512, 512), 7: (1024, 256)}
GATE_CHUNK0 = 8
N_CHUNKS = 12
CHUNK_COL = [0, 512, 1024, 1536, 2048, 2560, 3072, 3584, 3840, 4352, 4864, 5376]
QA, KA, QB, KB = 0, 4, 8, 14

C_ID, C_TRI, C_ONE, C_IOTA, C_EID, C_COS, C_SIN = 0, 128, 256, 384, 448, 449, 481
N_CONST = 513
MASK_A = [(0, 128), (128, 256)]
MASK_B = [(384, 384), (768, 768)]
N_MASK = 1536


def shape_constants():
    import numpy as np
    c = np.zeros((P, N_CONST), np.float32)
    row, col = np.arange(P)[:, None], np.arange(P)[None, :]
    c[:, C_ID:C_ID + P] = row == col
    c[:, C_TRI:C_TRI + P] = row < col
    c[:, C_ONE:C_ONE + P] = 1.0
    c[:, C_IOTA:C_IOTA + 64] = np.arange(64)
    c[:, C_EID] = np.arange(P)
    half = ROT // 2
    inv = np.float32(500000.0) ** (-np.arange(half, dtype=np.float32) / np.float32(half))
    for b in range(NB):
        ang = (np.arange(P) + P * b).astype(np.float32)[:, None] * inv.astype(np.float32)[None, :]
        cos, sin = np.cos(ang).astype(np.float32), np.sin(ang).astype(np.float32)
        c[:, C_COS + b * ROT:C_COS + (b + 1) * ROT] = np.concatenate([cos, cos], 1)
        c[:, C_SIN + b * ROT:C_SIN + (b + 1) * ROT] = np.concatenate([-sin, sin], 1)
    m = np.full((P, N_MASK), HIDE, np.float32)
    for b in range(NB):
        keys = P * (b + 1)
        back = (row + P * b) - np.arange(keys)[None, :]
        at = MASK_A[b][0]
        m[:, at:at + keys][back >= 0] = 0.0
        for g, dil in enumerate(DILATIONS):
            at = MASK_B[b][0] + g * keys
            m[:, at:at + keys][(back >= 0) & (back % dil == 0) & (back <= dil * BAND)] = 0.0
    return c, m


def layer(nc, x, ln_mix_g, w_in, b_gate_a, b_gate_b, w_o_a, w_o_b, w_out, ln_ffn_g, w_router, b_router,
          w_gate, b_gate, w_up, b_up, w_down, b_down, ln_final_g, consts, masks, out):
    ctx = ExitStack()

    def sb(name, shape, dt=F32):
        return ctx.enter_context(nc.sbuf_tensor(name, shape, dt))

    def sem(name):
        return ctx.enter_context(nc.semaphore(name))

    with ctx:
        wg = sb("wg", [P, KT, D])
        wu = sb("wu", [P, KT, D])
        wd = sb("wd", [P, KT, D])
        slots = [wu[:, 0:4, :], wu[:, 4:8, :], wd[:, 0:4, :], wd[:, 4:8, :]]
        slots = [s.rearrange("p a f -> p (a f)").rearrange("p (k c) -> p k c", c=CHUNK) for s in slots]
        woa = wu[:, 0:4, :]
        wob = wu[:, 4:6, :]
        wo = wd

        xs = sb("xs", [P, NB, D])
        xn = sb("xn", [P, NB, D])
        h_t = sb("h_t", [P, KT, SEQ])
        v_tok = sb("v_tok", [P, NB, 1280])
        qk_t = sb("qk_t", [P, 20, SEQ])
        mix_t = qk_t[:, 0:8, :]
        gates = sb("gates", [P, 2, KT, SEQ])
        o_t = sb("o_t", [P, 6, SEQ])
        work = sb("work", [P, 4608])
        stage = [work[:, 0:512], work[:, 512:1024]]
        rot_a = work[:, 1024:1152]
        rot_b = work[:, 1152:1280]
        probs = [work[:, 0:768], work[:, 768:1536]]
        masked = [work[:, 1536:2304], work[:, 2304:3072]]
        p_t = [work[:, 3072:3840], work[:, 3840:4608]]
        cst = sb("cst", [P, N_CONST])
        msk = sb("msk", [P, N_MASK])
        rows = sb("rows", [32, P])
        cols = sb("cols", [P, 32])
        bias_tab = sb("bias_tab", [P, D])
        b_dn = v_tok[0:E, 0, 0:D]
        w_rt = sb("w_rt", [P, KT, E])
        b_rt = sb("b_rt", [P, E])
        g_fin = msk[:, 0:D]
        stat = sb("stat", [P, 64])
        def tile2k(g, k):
            return gates[:, g, k:k + 2, :].rearrange("p a t -> p (a t)")

        x_rows, g_act, sig, u_act, a_rows = tile2k(0, 0), tile2k(0, 2), tile2k(0, 4), tile2k(0, 6), tile2k(1, 0)
        x_g = tile2k(1, 2).rearrange("p (k c) -> p k c", c=SLOTS)
        y_pair = gates[:, 1, 4:8, :].rearrange("p a t -> p (a t)")
        a_t = o_t[:, 0:2, :].rearrange("p a t -> p (a t)").rearrange("p (k c) -> p k c", c=SLOTS)
        sel_t = o_t[:, 2, :]
        sel = work[:, 0:128].rearrange("p (b c) -> p b c", c=SLOTS)
        pick_bias = work[:, 128:256].rearrange("p (m c) -> p m c", c=SLOTS)
        sel_p = work[:, 1536:1792].rearrange("p (b c) -> p b c", c=2 * SLOTS)
        iota_o = work[:, 256:320]
        pick = work[:, 512:640].rearrange("p (k e) -> p k e", e=E)
        pick_p = work[:, 640:768].rearrange("p (k e) -> p k e", e=E)
        logits = work[:, 768:832].rearrange("p (b e) -> p b e", e=E)
        chosen = work[:, 832:896].rearrange("p (b e) -> p b e", e=E)
        prob = work[:, 896:960].rearrange("p (b e) -> p b e", e=E)
        pos = work[:, 960:1024].rearrange("p (b e) -> p b e", e=E)
        prob_t = work[0:E, 1024:1280]
        tab = work[0:E, 1280:1344]
        offs = work[:, 1344:1360]
        top_v = work[:, 1400:1416]
        top_f = work[:, 1416:1424]
        top_e = work[:, 1424:1432]
        top_i = sb("top_i", [P, NB, 8], U32)
        over_i = sb("over_i", [1, 20], I32)

        ps = ctx.enter_context(nc.psum_tensor("ps", [P, 8, 512], F32))
        G, U, X, DN, Y = 0, 1, 2, 3, 4

        ident = cst[:, C_ID:C_ID + P]
        tri = cst[:, C_TRI:C_TRI + P]
        ones = cst[:, C_ONE:C_ONE + P]
        iota = cst[:, C_IOTA:C_IOTA + 64]

        ld_x = [sem(f"ld_x{b}") for b in range(NB)]
        ld_cst, ld_msk, ld_rows, ld_small = sem("ld_cst"), sem("ld_msk"), sem("ld_rows"), sem("ld_small")
        ld_chunk = [sem(f"ld_chunk{s}") for s in range(4)]
        ld_wo, ld_wout, ld_gfin, ld_bdn = sem("ld_wo"), sem("ld_wout"), sem("ld_gfin"), sem("ld_bdn")
        ld_piece = [sem(f"ld_piece{j}") for j in range(12)]
        oproj_done, wout_done = sem("oproj_done"), sem("wout_done")
        sq_done, var_ready, rstd_ready, xn_ready = sem("sq_done"), sem("var_ready"), sem("rstd_ready"), sem("xn_ready")
        neg_half = sem("neg_half")
        rows_turned, cols_ready = sem("rows_turned"), sem("cols_ready")
        x_turned, h_ready = sem("x_turned"), sem("h_ready")
        proj_done, proj_read = sem("proj_done"), sem("proj_read")
        rot_step, rotated = sem("rot_step"), sem("rotated")
        qk_turned, qk_ready = sem("qk_turned"), sem("qk_ready")
        scored, soft_step, row_max, exp_done, probs_ready = sem("scored"), sem("soft_step"), sem("row_max"), sem("exp_done"), sem("probs_ready")
        p_turned, p_ready = sem("p_turned"), sem("p_ready")
        pv_done, o_ready = sem("pv_done"), sem("o_ready")
        gate_done, gate_read = sem("gate_done"), sem("gate_read")
        gates_ready = sem("gates_ready")
        mix_step, mix_ready = sem("mix_step"), sem("mix_ready")
        res_ready = sem("res_ready")
        bias_zero = sem("bias_zero")
        logit_done, rt_step = sem("logit_done"), sem("rt_step")
        rt_exp_in, rt_exp = sem("rt_exp_in"), sem("rt_exp")
        chosen_ready, prob_ready = sem("chosen_ready"), sem("prob_ready")
        pos_done, prob_turned, prob_t_ready = sem("pos_done"), sem("prob_turned"), sem("prob_t_ready")
        count_done, nov_ready, ostart_done, tab_ready, tab_done, over_ready = (
            sem("count_done"), sem("nov_ready"), sem("ostart_done"), sem("tab_ready"), sem("tab_done"), sem("over_ready"))
        pieces_used = sem("pieces_used")
        sel_ready, gathered, x_rows_ready = sem("sel_ready"), sem("gathered"), sem("x_rows_ready")
        xg_turned, xg_ready = sem("xg_turned"), sem("xg_ready")
        g_ready, sig_done, act_ready = sem("g_ready"), sem("sig_done"), sem("act_ready")
        g_step, u_step, selp_step = sem("g_step"), sem("u_step"), sem("selp_step")
        a_turned, a_t_ready, y_ready = sem("a_turned"), sem("a_t_ready"), sem("y_ready")
        selp_ready, sel_turned, sel_t_ready = sem("selp_ready"), sem("sel_turned"), sem("sel_t_ready")
        combined = sem("combined")
        fin_step, fin_ready, stored = sem("fin_step"), sem("fin_ready"), sem("stored")

        x_v = x[0].rearrange("(b p) d -> b p d", p=P)
        out_v = out[0].rearrange("(b p) d -> b p d", p=P)
        win_v = w_in[0].rearrange("(k p) n -> p k n", p=P)
        row_v = [t[0].rearrange("(k p) -> k p", p=P) for t in (ln_mix_g, b_gate_a, b_gate_b, ln_ffn_g)]
        expert_v = [t[0].rearrange("e (k p) f -> e p k f", p=P) for t in (w_gate, w_up, w_down)]
        expert_sb = [wg, wu, wd]

        units = [("a", h, None) for h in range(HEADS_A)]
        units += [("b", j, b) for j in range(HEADS_G) for b in range(NB)]
        N_UNITS = len(units)

        def unit_rows(u):
            kind, h, b = units[u]
            if kind == "a":
                return [(0, 0, 128, MASK_A[0][0]), (1, 128, 256, MASK_A[1][0])]
            return [(b, 0, MASK_B[b][1], MASK_B[b][0])]

        def unit_blocks(u):
            kind, h, b = units[u]
            if kind == "a":
                return [(0, 0, 0, HD * h, True, True), (1, 128, 0, HD * h, True, False),
                        (1, 256, 1, HD * h, False, True)]
            last = NG * (b + 1) - 1
            return [(b, P * (g * (b + 1) + kb), kb, WIDTH_A + HD * (HEADS_G * g + h),
                     g == 0 and kb == 0, g * (b + 1) + kb == last) for g in range(NG) for kb in range(b + 1)]

        def unit_out(u):
            kind, h, b = units[u]
            return (h // 2 if kind == "a" else 4 + h // 2), h % 2

        def width(u):
            return len(unit_blocks(u)) * P

        n_soft = [sum(len(unit_rows(v)) for v in range(u)) for u in range(N_UNITS + 1)]
        closes = [(units[u][1] % 2 == 1 and units[u][2] in (None, 1)) for u in range(N_UNITS)]
        tile_end = [u for u in range(N_UNITS) if closes[u]]

        block = ctx.enter_context(nc.Block())

        @block.sync
        def _(sp):
            for b in range(NB):
                sp.dma_start(xs[:, b, :], x_v[b]).then_inc(ld_x[b], 16)

            def chunk(c):
                if c >= 4:
                    sp.wait_ge(proj_done, NB * (c - 3))
                n = V_CHUNKS[c][1] if c in V_CHUNKS else CHUNK
                sp.dma_start(slots[c % 4][:, :, 0:n], win_v[:, :, CHUNK_COL[c]:CHUNK_COL[c] + n])\
                  .then_inc(ld_chunk[c % 4], 16)

            def piece(m, j, e, s):
                sp.dma_start(expert_sb[m][:, 2 * j:2 * j + 2, :], expert_v[m][e, :, 2 * j:2 * j + 2, :])\
                  .then_inc(s, 16)

            for c in range(5):
                chunk(c)
            sp.dma_start(msk[:], masks).then_inc(ld_msk, 16)
            for c in range(5, N_CHUNKS):
                if c < 9:
                    piece(0, c - 5, 0, ld_piece[c - 5])
                chunk(c)
            sp.wait_ge(gate_done, 8)
            sp.dma_start(woa, w_o_a[0].rearrange("(k p) n -> p k n", p=P)).then_inc(ld_wo, 16)
            sp.dma_start(wob, w_o_b[0].rearrange("(k p) n -> p k n", p=P)).then_inc(ld_wo, 16)
            sp.wait_ge(gate_done, 16)
            sp.dma_start(wo[:], w_out[0].rearrange("(k p) n -> p k n", p=P)).then_inc(ld_wout, 16)
            sp.wait_ge(oproj_done, 8)
            for j in range(4):
                piece(1, j, 0, ld_piece[4 + j])
            sp.dma_start(b_dn, b_down[0]).then_inc(ld_bdn, 16)
            sp.wait_ge(wout_done, 4)
            for j in range(4):
                piece(2, j, 0, ld_piece[8 + j])

            sp.dma_start(g_fin, ln_final_g.rearrange("(a d) -> a d", a=1).broadcast_to([P, D])).then_inc(ld_gfin, 16)

            def item_loads(n, e):
                for q in range(12):
                    sp.wait_ge(pieces_used, 12 * n - 11 + q)
                    piece(q // 4, q % 4, e, ld_piece[q])

            with sp.Fori(1, E) as i:
                item_loads(i, i)
            sp.wait_ge(over_ready, 1)
            count = sp.value_load(over_i[0:1, 16:17], min_val=0, max_val=MAX_OVER)
            with sp.If(count > 0):
                with sp.Fori(0, count) as k:
                    e = sp.value_load(over_i[0:1, bass.ds(k, 1)], min_val=0, max_val=E - 1)
                    item_loads(k + E, e)
            for b in range(NB):
                sp.wait_ge(fin_ready, b + 1)
                sp.dma_start(out_v[b], xn[:, b, :]).then_inc(stored, 16)
            sp.wait_ge(stored, 16 * NB)

        @block.gpsimd
        def _(pool):
            pool.memset(bias_tab[2 * E:P, :], 0.0).then_inc(bias_zero, 1)
            pool.wait_ge(bias_zero, 1)
            pool.memset(stat[:, 60:62], -0.5).then_inc(neg_half, 1)
            pool.wait_ge(neg_half, 1)
            for n in range(3 * NB):
                pool.wait_ge(var_ready, n + 1)
                pool.tensor_tensor(stat[:, 12 + n:13 + n], stat[:, 6 + n:7 + n], stat[:, 60:61], ALU.pow)\
                    .then_inc(rstd_ready, 1)

        @block.scalar
        def _(act):
            act.dma_start(cst[:], consts).then_inc(ld_cst, 16)
            for r in range(4):
                act.dma_start(rows[8 * r:8 * r + 8, :], row_v[r]).then_inc(ld_rows, 16)
            act.dma_start(bias_tab[0:E, :], b_gate[0]).then_inc(ld_small, 16)
            act.dma_start(bias_tab[E:2 * E, :], b_up[0]).then_inc(ld_small, 16)
            act.dma_start(w_rt[:], w_router[0].rearrange("(k p) e -> p k e", p=P)).then_inc(ld_small, 16)
            act.dma_start(b_rt[:], b_router.broadcast_to([P, E])).then_inc(ld_small, 16)

            for b in range(NB):
                act.wait_ge(ld_x[b], 16)
                act.activation(h_t[:, 4 * b:4 * b + 4, :].rearrange("p k t -> p (k t)"), xs[:, b, :], ACT.Square,
                               accum_out=stat[:, b:b + 1]).then_inc(sq_done, 1)

            qk_seen = 0
            for c in range(8):
                for b in range(NB):
                    act.wait_ge(proj_done, NB * c + b + 1)
                    if c in QK_CHUNKS:
                        if qk_seen >= 2:
                            act.wait_ge(qk_turned, qk_seen - 1)
                        act.activation(stage[b], ps[:, b, :], ACT.Copy).then_inc(proj_read, 1)
                        qk_seen += 1
                    else:
                        at, n = V_CHUNKS[c]
                        act.activation(v_tok[:, b, at:at + n], ps[:, b, 0:n], ACT.Copy).then_inc(proj_read, 1)

            def evac_gate(t):
                act.wait_ge(gate_done, t + 1)
                act.activation(gates[:, t // 8, t % 8, :], ps[:, t % 2, 0:SEQ], ACT.Identity,
                               bias=cols[:, 8 + t:9 + t]).then_inc(gate_read, 1)

            def exps(u):
                for n, (b, at, w, _m) in enumerate(unit_rows(u)):
                    s = n_soft[u] + n
                    act.wait_ge(row_max, s + 1)
                    act.activation(probs[u % 2][:, at:at + w], masked[u % 2][:, at:at + w], ACT.Exp,
                                   bias=stat[:, 20 + (s % 4):21 + (s % 4)], scale=SCALE,
                                   accum_out=stat[:, 24 + (s % 4):25 + (s % 4)]).then_inc(exp_done, 1)

            def evac_o(t):
                act.wait_ge(pv_done, tile_end[t] + 1)
                act.activation(o_t[:, t, :], ps[:, 6 + t % 2, 0:SEQ], ACT.Copy).then_inc(o_ready, 1)

            act.wait_ge(cols_ready, 1)
            tiles_out = 0
            for u in range(N_UNITS):
                if u >= 2:
                    act.wait_ge(p_turned, u - 1)
                exps(u)
                evac_gate(u)
                while tiles_out < len(tile_end) and tile_end[tiles_out] <= u - 2:
                    evac_o(tiles_out)
                    tiles_out += 1
            while tiles_out < len(tile_end):
                evac_o(tiles_out)
                tiles_out += 1
            act.wait_ge(gate_read, 16)
            for g in range(2):
                v = gates[:, g, :, :].rearrange("p k t -> p (k t)")
                act.activation(v, v, ACT.Sigmoid).then_inc(gates_ready, 1)

            for b in range(NB):
                act.wait_ge(rt_exp_in, b + 1)
                act.activation(top_e[:, 4 * b:4 * b + 4], top_v[:, 8 * b:8 * b + 4], ACT.Exp,
                               bias=stat[:, 30 + b:31 + b], accum_out=stat[:, 32 + b:33 + b]).then_inc(rt_exp, 1)
            act.wait_ge(prob_turned, 1)
            act.activation(prob_t, ps[0:E, DN, 0:SEQ], ACT.Copy).then_inc(prob_t_ready, 1)

            def item_sigmoid(n):
                act.wait_ge(g_ready, n + 1)
                act.activation(sig, g_act, ACT.Sigmoid, scale=ALPHA).then_inc(sig_done, 1)

            def turned_selection(pairs):
                act.wait_ge(sel_turned, pairs)
                act.activation(sel_t, ps[:, DN, 0:SEQ], ACT.Copy).then_inc(sel_t_ready, 1)

            def gathered_out(n):
                act.wait_ge(gathered, n + 1)
                act.activation(x_rows, ps[:, X, :], ACT.Copy).then_inc(x_rows_ready, 1)

            def turned_activation(n):
                act.wait_ge(a_turned, n + 1)
                act.activation(a_t.rearrange("p (h j) c -> p j h c", h=2),
                               ps[:, G, :].rearrange("p (j h c) -> p j h c", h=2, c=SLOTS), ACT.Copy)\
                   .then_inc(a_t_ready, 1)

            def item_out(n, side):
                act.wait_ge(pieces_used, n * 12 + 12)
                for h in range(2):
                    act.activation(y_pair[SLOTS * side:SLOTS * side + SLOTS, 512 * h:512 * h + 512],
                                   ps[SLOTS * h:SLOTS * h + SLOTS, DN, :], ACT.Copy).then_inc(y_ready, 1)

            def pair(i, first=False, last=False):
                for side in range(2):
                    n = i * 2 + side
                    item_sigmoid(n)
                    if not (last and side):
                        gathered_out(n + 1)
                    if side == 0 and not first:
                        turned_selection(i)
                    turned_activation(n)
                    item_out(n, side)

            gathered_out(0)
            pair(0, first=True)
            with act.Fori(1, E // 2 - 1) as i:
                pair(i)
            pair(E // 2 - 1, last=True)
            turned_selection(E // 2)
            act.wait_ge(over_ready, 1)
            count = act.value_load(over_i[0:1, 16:17], min_val=0, max_val=MAX_OVER)
            with act.If(count > 0):
                with act.Fori(0, count) as k:
                    n = k + E
                    gathered_out(n)
                    item_sigmoid(n)
                    turned_activation(n)
                    item_out(n, 0)
                    turned_selection(k + (E // 2 + 1))

        @block.tensor
        def _(pe):
            def turn(out_ap, in_ap):
                n = in_ap.shape[0]
                return pe.transpose(out_ap, in_ap, ident[0:n, 0:n])

            pe.wait_ge(ld_cst, 16)
            pe.wait_ge(ld_rows, 64)
            turn(ps[:, 6, 0:32], rows[:]).then_inc(rows_turned, 1)
            for b in range(NB):
                pe.wait_ge(xn_ready, b + 1)
                for h in range(2):
                    for k in range(4):
                        mm = turn(ps[:, 2 + 2 * b + h, P * k:P * k + P], xn[:, b, P * (4 * h + k):P * (4 * h + k) + P])
                    mm.then_inc(x_turned, 1)

            qk_turns = 0

            def turn_qk(c):
                nonlocal qk_turns
                for b in range(NB):
                    pe.wait_ge(rotated, qk_turns + 1)
                    if qk_turns >= 2:
                        pe.wait_ge(qk_ready, qk_turns - 1)
                    for k in range(4):
                        mm = turn(ps[:, 2 + b, P * k:P * k + P], stage[b][:, P * k:P * k + P])
                    mm.then_inc(qk_turned, 1)
                    qk_turns += 1

            for c in range(8):
                pe.wait_ge(ld_chunk[c % 4], 16 * (c // 4 + 1))
                n = V_CHUNKS[c][1] if c in V_CHUNKS else CHUNK
                for b in range(NB):
                    if c == 0:
                        pe.wait_ge(h_ready, 2 * (b + 1))
                    else:
                        pe.wait_ge(proj_read, NB * (c - 1) + b + 1)
                    for k in range(KT):
                        mm = pe.matmul(ps[:, b, 0:n], h_t[:, k, P * b:P * b + P], slots[c % 4][:, k, 0:n],
                                       start=(k == 0), stop=(k == KT - 1))
                    mm.then_inc(proj_done, 1)
                if c >= 1 and (c - 1) in QK_CHUNKS:
                    turn_qk(c - 1)

            def scores(u):
                kind, h, b = units[u]
                base = 2 + 2 * (u % 2)
                if u >= 2:
                    pe.wait_ge(p_ready, u - 1)
                if kind == "a":
                    r = HD * (h % 2)
                    q, k = qk_t[r:r + HD, QA + h // 2, :], qk_t[r:r + HD, KA + h // 2, :]
                    pe.matmul(ps[:, base, 0:128], q[:, 0:128], k[:, 0:128], start=True, stop=True)
                    mm = pe.matmul(ps[:, base, 128:384], q[:, 128:256], k[:, 0:256], start=True, stop=True)
                else:
                    keys = P * (b + 1)
                    for g in range(NG):
                        hh = HEADS_G * g + h
                        r = HD * (hh % 2)
                        q, k = qk_t[r:r + HD, QB + hh // 2, :], qk_t[r:r + HD, KB + hh // 2, :]
                        at = g * keys
                        mm = pe.matmul(ps[:, base + at // 512, at % 512:at % 512 + keys], q[:, P * b:P * b + P],
                                       k[:, 0:keys], start=True, stop=True)
                mm.then_inc(scored, 1)

            def gate_tile(t):
                c = GATE_CHUNK0 + t // 4
                if t % 4 == 0:
                    pe.wait_ge(ld_chunk[c % 4], 16 * (c // 4 + 1))
                if t >= 2:
                    pe.wait_ge(gate_read, t - 1)
                else:
                    pe.wait_ge(proj_read, 16)
                for k in range(KT):
                    mm = pe.matmul(ps[:, t % 2, 0:SEQ], slots[c % 4][:, k, P * (t % 4):P * (t % 4) + P],
                                   h_t[:, k, :], start=(k == 0), stop=(k == KT - 1))
                mm.then_inc(gate_done, 1)

            def turn_probs(u):
                base = 2 + 2 * (u % 2)
                pe.wait_ge(probs_ready, n_soft[u + 1])
                for (_b, at, _k, _v, _f, _l) in unit_blocks(u):
                    mm = turn(ps[:, base + at // 512, at % 512:at % 512 + P], probs[u % 2][:, at:at + P])
                mm.then_inc(p_turned, 1)

            def weigh_values(u):
                t, half = unit_out(u)
                pe.wait_ge(p_ready, u + 1)
                if t >= 2:
                    pe.wait_ge(o_ready, t - 1)
                for (b, at, kb, v, first, last) in unit_blocks(u):
                    mm = pe.matmul(ps[HD * half:HD * half + HD, 6 + t % 2, P * b:P * b + P],
                                   v_tok[:, kb, v:v + HD], p_t[u % 2][:, at:at + P], start=first, stop=last)
                mm.then_inc(pv_done, 1)

            pe.wait_ge(qk_ready, 10)
            pe.wait_ge(cols_ready, 1)
            scores(0)
            for u in range(N_UNITS):
                gate_tile(u)
                if u + 1 < N_UNITS:
                    scores(u + 1)
                turn_probs(u)
                if u >= 1:
                    weigh_values(u - 1)
            weigh_values(N_UNITS - 1)

            pe.wait_ge(ld_wo, 32)
            pe.wait_ge(o_ready, 6)
            for m in range(KT):
                if m < 2:
                    pe.wait_ge(gate_read, 15 + m)
                else:
                    pe.wait_ge(mix_ready, m - 1)
                for k in range(4):
                    pe.matmul(ps[:, m % 2, 0:SEQ], woa[:, k, P * m:P * m + P], o_t[:, k, :],
                              start=(k == 0), stop=(k == 3))
                for k in range(2):
                    mm = pe.matmul(ps[:, m % 2, SEQ:2 * SEQ], wob[:, k, P * m:P * m + P], o_t[:, 4 + k, :],
                                   start=(k == 0), stop=(k == 1))
                mm.then_inc(oproj_done, 1)
            pe.wait_ge(ld_wout, 16)
            for b in range(NB):
                for h in range(2):
                    for k in range(KT):
                        pe.wait_ge(mix_ready, k + 1) if b == 0 and h == 0 else None
                        mm = pe.matmul(ps[:, 2 + 2 * b + h, :], mix_t[:, k, P * b:P * b + P],
                                       wo[:, k, 512 * h:512 * h + 512], start=(k == 0), stop=(k == KT - 1))
                    mm.then_inc(wout_done, 1)

            pe.wait_ge(ld_small, 16 * 4)
            pe.wait_ge(bias_zero, 1)
            for b in range(NB):
                pe.wait_ge(xn_ready, NB + b + 1)
                for h in range(2):
                    if b == 1:
                        pe.wait_ge(h_ready, 4 + h + 1)
                    for k in range(4):
                        mm = turn(ps[:, 6 + h, P * k:P * k + P], xn[:, b, P * (4 * h + k):P * (4 * h + k) + P])
                    mm.then_inc(x_turned, 1)
                pe.wait_ge(h_ready, 4 + 2 * b + 2)
                for k in range(KT):
                    mm = pe.matmul(ps[:, b, 0:E], h_t[:, k, P * b:P * b + P], w_rt[:, k, :],
                                   start=(k == 0), stop=(k == KT - 1))
                mm.then_inc(logit_done, 1)
            pe.wait_ge(chosen_ready, 2)
            pe.matmul(ps[:, U, 0:E], tri, chosen[:, 0, :], start=True, stop=True)
            pe.matmul(ps[:, U, E:2 * E], ones, chosen[:, 0, :], start=True, stop=False)
            pe.matmul(ps[:, U, E:2 * E], tri, chosen[:, 1, :], start=False, stop=True).then_inc(pos_done, 1)
            for b in range(NB):
                mm = pe.matmul(ps[0:E, G, 0:1], chosen[:, b, :], ones[:, 0:1], start=(b == 0), stop=(b == NB - 1))
            mm.then_inc(count_done, 1)
            pe.wait_ge(prob_ready, 2)
            for b in range(NB):
                mm = turn(ps[0:E, DN, P * b:P * b + P], prob[:, b, :])
            mm.then_inc(prob_turned, 1)

            def gather(n):
                pe.wait_ge(sel_ready, n + 1)
                for b in range(NB):
                    for h in range(2):
                        mm = pe.matmul(ps[SLOTS * h:SLOTS * h + SLOTS, X, :], sel[:, b, :],
                                       xn[:, b, 512 * h:512 * h + 512], start=(b == 0), stop=(b == NB - 1),
                                       skip_group_check=True)
                mm.then_inc(gathered, 1)

            def turn_rows(bank, rows_ap):
                for j in range(4):
                    mm = turn(ps[:, bank, P * j:P * j + P], rows_ap[:, P * j:P * j + P])
                return mm

            def turn_gathered(n):
                pe.wait_ge(x_rows_ready, n + 1)
                turn_rows(X, x_rows).then_inc(xg_turned, 1)

            def turn_activation(n):
                pe.wait_ge(act_ready, n + 1)
                turn_rows(G, a_rows).then_inc(a_turned, 1)

            def product(m, n, bank, lhs, bias=True):
                if bias:
                    for h in range(2):
                        pe.matmul(ps[SLOTS * h:SLOTS * h + SLOTS, bank, :], pick_bias[:, m, :],
                                  bias_tab[:, 512 * h:512 * h + 512], start=True, stop=False, skip_group_check=True)
                for j in range(4):
                    pe.wait_ge(ld_piece[4 * m + j], n * 16 + 16)
                    for k in (2 * j, 2 * j + 1):
                        for h in range(2):
                            mm = pe.matmul(ps[SLOTS * h:SLOTS * h + SLOTS, bank, :], lhs[:, k, :],
                                           expert_sb[m][:, k, 512 * h:512 * h + 512],
                                           start=(k == 0 and not bias), stop=(k == KT - 1), skip_group_check=True)
                    mm.then_inc(pieces_used, 1)

            def gate_and_up(n):
                pe.wait_ge(xg_ready, n + 1)
                product(0, n, G, x_g)
                product(1, n, U, x_g)

            def turn_selection(pairs, outputs):
                pe.wait_ge(y_ready, outputs)
                pe.wait_ge(selp_ready, pairs)
                for b in range(NB):
                    mm = turn(ps[:, DN, P * b:P * b + P], sel_p[:, b, :])
                mm.then_inc(sel_turned, 1)

            def combine(pairs, slots):
                pe.wait_ge(sel_t_ready, pairs)
                for h in range(2):
                    for b in range(NB):
                        mm = pe.matmul(ps[:, Y + 2 * b + h, :], sel_t[0:slots, P * b:P * b + P],
                                       y_pair[0:slots, 512 * h:512 * h + 512], start=False, stop=False,
                                       skip_group_check=True)
                mm.then_inc(combined, 1)

            gather(0)
            pe.wait_ge(prob_t_ready, 1)
            pe.wait_ge(ld_bdn, 16)
            pe.wait_ge(res_ready, 4)
            for b in range(NB):
                for h in range(2):
                    pe.matmul(ps[:, Y + 2 * b + h, :], prob_t[:, P * b:P * b + P], b_dn[:, 512 * h:512 * h + 512],
                              start=True, stop=False, skip_group_check=True)
            turn_gathered(0)
            pe.wait_ge(nov_ready, 1)
            pe.matmul(ps[0:E, DN, 0:1], tri[0:E, 0:E], tab[:, 32:33], start=True, stop=True).then_inc(ostart_done, 1)

            def pair(i, first=False, last=False):
                for side in range(2):
                    n = i * 2 + side
                    gate_and_up(n)
                    if not (last and side):
                        gather(n + 1)
                    if side == 0 and first:
                        pe.wait_ge(tab_ready, 1)
                        pe.matmul(ps[:, DN, 0:33], ones[0:E, :], tab[:, 0:33], start=True, stop=True).then_inc(tab_done, 1)
                    elif side == 0:
                        turn_selection(i, i * 4)
                        combine(i, P)
                    if not (last and side):
                        turn_gathered(n + 1)
                    turn_activation(n)
                    if side == 0 and first:
                        pe.wait_ge(over_ready, 1)
                    elif side == 1:
                        pe.wait_ge(y_ready, i * 4 + 2)
                    pe.wait_ge(a_t_ready, n + 1)
                    product(2, n, DN, a_t, bias=False)

            pair(0, first=True)
            with pe.Fori(1, E // 2 - 1) as i:
                pair(i)
            pair(E // 2 - 1, last=True)
            turn_selection(E // 2, 2 * E)
            combine(E // 2, P)

            count = pe.value_load(over_i[0:1, 16:17], min_val=0, max_val=MAX_OVER)
            with pe.If(count > 0):
                with pe.Fori(0, count) as k:
                    n = k + E
                    gather(n)
                    turn_gathered(n)
                    gate_and_up(n)
                    turn_activation(n)
                    pe.wait_ge(a_t_ready, n + 1)
                    product(2, n, DN, a_t, bias=False)
                    turn_selection(k + (E // 2 + 1), n * 2 + 2)
                    combine(k + (E // 2 + 1), SLOTS)

        @block.vector
        def _(dve):
            def variance(n):
                dve.tensor_scalar(stat[:, 6 + n:7 + n], stat[:, n:n + 1], 1.0 / D, EPS, ALU.mult, ALU.add)\
                   .then_inc(var_ready, 1)

            def normalise(n, b):
                dve.wait_ge(rstd_ready, n + 1)
                dve.tensor_scalar(xn[:, b, :], xs[:, b, :], stat[:, 12 + n:13 + n], None, ALU.mult)\
                   .then_inc(xn_ready, 1)

            dve.wait_ge(rows_turned, 1)
            dve.tensor_copy(cols[:], ps[:, 6, 0:32]).then_inc(cols_ready, 1)
            for b in range(NB):
                dve.wait_ge(sq_done, b + 1)
                variance(b)
            for b in range(NB):
                normalise(b, b)
            dve.wait_ge(cols_ready, 1)

            def spread(col, n):
                return col.rearrange("p (k a) -> p k a", a=1).broadcast_to([P, n[0], n[1]])

            for b in range(NB):
                for h in range(2):
                    dve.wait_ge(x_turned, 2 * b + h + 1)
                    if b == 0 and h == 0:
                        dve.wait_ge(sq_done, 2)
                    dve.tensor_tensor(h_t[:, 4 * h:4 * h + 4, P * b:P * b + P],
                                      ps[:, 2 + 2 * b + h, :].rearrange("p (k t) -> p k t", t=P),
                                      spread(cols[:, 4 * h:4 * h + 4], (4, P)), ALU.mult).then_inc(h_ready, 1)

            steps = 0
            seen = 0
            turned_out = 0

            def qk_out(c):
                nonlocal turned_out
                t0 = QK_CHUNKS[c]
                for b in range(NB):
                    dve.wait_ge(qk_turned, turned_out + 1)
                    dve.tensor_copy(qk_t[:, t0:t0 + 4, P * b:P * b + P],
                                    ps[:, 2 + b, :].rearrange("p (k t) -> p k t", t=P)).then_inc(qk_ready, 1)
                    turned_out += 1

            for c in range(8):
                if c in QK_CHUNKS:
                    for b in range(NB):
                        dve.wait_ge(proj_read, NB * c + b + 1)
                        s = stage[b].rearrange("p (h d) -> p h d", d=HD)
                        ra = rot_a.rearrange("p (h d) -> p h d", d=ROT)
                        rb = rot_b.rearrange("p (h d) -> p h d", d=ROT)
                        cos = cst[:, C_COS + ROT * b:C_COS + ROT * b + ROT].rearrange("p (a d) -> p a d", a=1)
                        sin = cst[:, C_SIN + ROT * b:C_SIN + ROT * b + ROT].rearrange("p (a d) -> p a d", a=1)
                        if steps:
                            dve.wait_ge(rotated, seen)
                        dve.tensor_tensor(ra, s[:, :, 0:ROT], cos.broadcast_to([P, 8, ROT]), ALU.mult).then_inc(rot_step, 1)
                        dve.tensor_tensor(rb[:, :, 0:8], s[:, :, 8:16], sin[:, :, 0:8].broadcast_to([P, 8, 8]), ALU.mult)\
                           .then_inc(rot_step, 1)
                        dve.tensor_tensor(rb[:, :, 8:16], s[:, :, 0:8], sin[:, :, 8:16].broadcast_to([P, 8, 8]), ALU.mult)\
                           .then_inc(rot_step, 1)
                        steps += 3
                        dve.wait_ge(rot_step, steps)
                        dve.tensor_tensor(s[:, :, 0:ROT], ra, rb, ALU.add).then_inc(rotated, 1)
                        seen += 1
                if c >= 1 and (c - 1) in QK_CHUNKS:
                    qk_out(c - 1)

            dve.wait_ge(ld_msk, 16)
            dve.wait_ge(qk_turned, 10)
            soft_steps = 0

            def row_maxima(u):
                nonlocal soft_steps
                base = 2 + 2 * (u % 2)
                flat = ps[:, base:base + 2, :].rearrange("p a c -> p (a c)")
                dve.wait_ge(scored, u + 1)
                if u >= 2:
                    dve.wait_ge(exp_done, n_soft[u - 1])
                for n, (b, at, w, mk) in enumerate(unit_rows(u)):
                    s = n_soft[u] + n
                    dve.tensor_tensor_reduce(masked[u % 2][:, at:at + w], flat[:, at:at + w], msk[:, mk:mk + w],
                                             1.0, HIDE, ALU.add, ALU.max, stat[:, 28 + n:29 + n]).then_inc(soft_step, 1)
                    soft_steps += 1
                    dve.wait_ge(soft_step, soft_steps)
                    if s >= 4:
                        dve.wait_ge(exp_done, s - 3)
                    dve.tensor_scalar(stat[:, 20 + (s % 4):21 + (s % 4)], stat[:, 28 + n:29 + n], -SCALE, None, ALU.mult)\
                       .then_inc(row_max, 1)

            def divide(u):
                nonlocal soft_steps
                for n, (b, at, w, _m) in enumerate(unit_rows(u)):
                    s = n_soft[u] + n
                    dve.wait_ge(exp_done, s + 1)
                    dve.reciprocal(stat[:, 34 + (s % 4):35 + (s % 4)], stat[:, 24 + (s % 4):25 + (s % 4)]).then_inc(soft_step, 1)
                    soft_steps += 1
                    dve.wait_ge(soft_step, soft_steps)
                    pr = probs[u % 2][:, at:at + w]
                    dve.tensor_scalar(pr, pr, stat[:, 34 + (s % 4):35 + (s % 4)], None, ALU.mult).then_inc(probs_ready, 1)

            def probs_out(u):
                base = 2 + 2 * (u % 2)
                w = width(u)
                dve.wait_ge(p_turned, u + 1)
                if u >= 2:
                    dve.wait_ge(pv_done, u - 1)
                dve.tensor_copy(p_t[u % 2][:, 0:w], ps[:, base:base + 2, :].rearrange("p a c -> p (a c)")[:, 0:w])\
                   .then_inc(p_ready, 1)

            row_maxima(0)
            for u in range(N_UNITS):
                divide(u)
                if u + 1 < N_UNITS:
                    row_maxima(u + 1)
                probs_out(u)

            dve.wait_ge(gates_ready, 2)
            for m in range(KT):
                dve.wait_ge(oproj_done, m + 1)
                ta, tb = work[:, 512 * (m % 2):512 * (m % 2) + 256], work[:, 512 * (m % 2) + 256:512 * (m % 2) + 512]
                dve.tensor_tensor(ta, ps[:, m % 2, 0:SEQ], gates[:, 0, m, :], ALU.mult).then_inc(mix_step, 1)
                dve.tensor_tensor(tb, ps[:, m % 2, SEQ:2 * SEQ], gates[:, 1, m, :], ALU.mult).then_inc(mix_step, 1)
                dve.wait_ge(mix_step, 2 * m + 2)
                dve.tensor_tensor(mix_t[:, m, :], ta, tb, ALU.add).then_inc(mix_ready, 1)
            dve.wait_ge(mix_ready, KT)

            for b in range(NB):
                for h in range(2):
                    q = slice(512 * h, 512 * h + 512)
                    dve.wait_ge(wout_done, 2 * b + h + 1)
                    dve.tensor_tensor(xs[:, b, q], xs[:, b, q], ps[:, 2 + 2 * b + h, :], ALU.add).then_inc(res_ready, 1)
                dve.wait_ge(res_ready, 2 * b + 2)
                dve.tensor_tensor_reduce(work[:, 1024:2048], xs[:, b, :], xs[:, b, :], 1.0, 0.0, ALU.mult, ALU.add,
                                         stat[:, 2 + b:3 + b]).then_inc(sq_done, 1)
                dve.wait_ge(sq_done, NB + b + 1)
                variance(NB + b)
                normalise(NB + b, b)

            rt = 0

            def step(ins):
                nonlocal rt
                rt += 1
                ins.then_inc(rt_step, 1)
                dve.wait_ge(rt_step, rt)

            for b in range(NB):
                for h in range(2):
                    dve.wait_ge(x_turned, 4 + 2 * b + h + 1)
                    dve.tensor_tensor(h_t[:, 4 * h:4 * h + 4, P * b:P * b + P],
                                      ps[:, 6 + h, :].rearrange("p (k t) -> p k t", t=P),
                                      spread(cols[:, 24 + 4 * h:24 + 4 * h + 4], (4, P)), ALU.mult).then_inc(h_ready, 1)
            for b in range(NB):
                dve.wait_ge(logit_done, b + 1)
                lg, tv = logits[:, b, :], top_v[:, 8 * b:8 * b + 8]
                step(dve.tensor_tensor(lg, ps[:, b, 0:E], b_rt[:], ALU.add))
                step(dve.max(tv, lg))
                dve.tensor_scalar(stat[:, 30 + b:31 + b], tv[:, 0:1], -1.0, None, ALU.mult).then_inc(rt_exp_in, 1)
                step(dve.max_index(top_i[:, b, :], tv, lg))
                step(dve.tensor_copy(top_f[:, 4 * b:4 * b + 4], top_i[:, b, 0:4]))
                step(dve.tensor_tensor(pick, iota[:, 0:E].rearrange("p (a e) -> p a e", a=1).broadcast_to([P, TOP_K, E]),
                                       spread(top_f[:, 4 * b:4 * b + 4], (TOP_K, E)), ALU.is_equal))
                dve.tensor_reduce(chosen[:, b, :], pick.rearrange("p k e -> p e k"), AX.X, ALU.add).then_inc(chosen_ready, 1)
                dve.wait_ge(rt_exp, b + 1)
                step(dve.reciprocal(stat[:, 40 + b:41 + b], stat[:, 32 + b:33 + b]))
                step(dve.tensor_scalar(top_e[:, 4 * b:4 * b + 4], top_e[:, 4 * b:4 * b + 4], stat[:, 40 + b:41 + b], None, ALU.mult))
                step(dve.tensor_tensor(pick_p, pick, spread(top_e[:, 4 * b:4 * b + 4], (TOP_K, E)), ALU.mult))
                dve.tensor_reduce(prob[:, b, :], pick_p.rearrange("p k e -> p e k"), AX.X, ALU.add).then_inc(prob_ready, 1)
                dve.wait_ge(prob_ready, b + 1)
            dve.wait_ge(chosen_ready, 2)
            step(dve.tensor_scalar(pos, chosen, FAR, -FAR, ALU.mult, ALU.add))
            dve.wait_ge(pos_done, 1)
            step(dve.tensor_tensor(pos, pos, ps[:, U, 0:2 * E].rearrange("p (b e) -> p b e", e=E), ALU.add))

            gain = cols[:, 24:32].rearrange("p (h j a) -> p j h a", h=2, a=1).broadcast_to([P, 4, 2, SLOTS])
            iota_b = iota.rearrange("p (a c) -> p a c", a=1).broadcast_to([P, NB, SLOTS])

            def at_expert(tab_ap, e):
                return tab_ap[:, :, bass.ds(e, 1)].broadcast_to([P, NB, SLOTS])

            def select(e, slot_ids=iota_b):
                for m in range(2):
                    dve.tensor_copy(pick_bias[:, m, :], ident[:, bass.ds(e + E * m, 1)].broadcast_to([P, SLOTS]))
                dve.tensor_tensor(sel, slot_ids, at_expert(pos, e), ALU.is_equal).then_inc(sel_ready, 1)

            def select_p(steps, side, e, slot_ids=iota_b):
                half = sel_p[:, :, SLOTS * side:SLOTS * side + SLOTS]
                dve.tensor_tensor(half, slot_ids, at_expert(pos, e), ALU.is_equal).then_inc(selp_step, 1)
                dve.wait_ge(selp_step, steps)
                return dve.tensor_tensor(half, half, at_expert(prob, e), ALU.mult)

            def select_pair(i):
                for side in range(2):
                    ins = select_p(i * 2 + (side + 1), side, i * 2 + side)
                ins.then_inc(selp_ready, 1)

            def gathered_out(n):
                dve.wait_ge(xg_turned, n + 1)
                dve.tensor_tensor(x_g.rearrange("p (h j) c -> p j h c", h=2),
                                  ps[:, X, :].rearrange("p (j h c) -> p j h c", h=2, c=SLOTS),
                                  gain, ALU.mult).then_inc(xg_ready, 1)

            def gate_part(n):
                dve.wait_ge(pieces_used, n * 12 + 4)
                dve.tensor_scalar(g_act, ps[:, G, :], LIMIT, None, ALU.min).then_inc(g_ready, 1)
                dve.wait_ge(sig_done, n + 1)
                dve.tensor_tensor(g_act, g_act, sig, ALU.mult).then_inc(g_step, 1)

            def up_part(n):
                dve.wait_ge(pieces_used, n * 12 + 8)
                dve.tensor_scalar(u_act, ps[:, U, :], LIMIT, -LIMIT, ALU.min, ALU.max).then_inc(u_step, 1)
                dve.wait_ge(u_step, n + 1)
                dve.wait_ge(g_step, n + 1)
                dve.scalar_tensor_tensor(a_rows, u_act, 1.0, g_act, ALU.add, ALU.mult).then_inc(act_ready, 1)

            select(0)
            dve.wait_ge(count_done, 1)
            cnt = ps[0:E, G, 0:1]
            step(dve.tensor_scalar(tab[:, 33:34], cnt, float(SLOTS), None, ALU.is_gt))
            step(dve.tensor_scalar(tab[:, 34:35], cnt, float(2 * SLOTS), None, ALU.is_gt))
            step(dve.tensor_scalar(tab[:, 35:36], cnt, float(3 * SLOTS), None, ALU.is_gt))
            dve.tensor_reduce(tab[:, 32:33], tab[:, 33:36], AX.X, ALU.add).then_inc(nov_ready, 1)
            dve.wait_ge(nov_ready, 1)
            gathered_out(0)
            dve.wait_ge(ostart_done, 1)
            step(dve.tensor_scalar(tab[:, 36:52], iota[0:E, 0:16], ps[0:E, DN, 0:1], None, ALU.subtract))
            step(dve.tensor_scalar(tab[:, 0:16], tab[:, 36:52], tab[:, 32:33], None, ALU.is_lt))
            step(dve.tensor_scalar(tab[:, 16:32], tab[:, 36:52], 0.0, None, ALU.is_ge))
            step(dve.tensor_tensor(tab[:, 16:32], tab[:, 0:16], tab[:, 16:32], ALU.mult))
            step(dve.tensor_scalar(tab[:, 36:52], tab[:, 36:52], 1.0, float(SLOTS), ALU.add, ALU.mult))
            step(dve.tensor_tensor(tab[:, 0:16], tab[:, 36:52], tab[:, 16:32], ALU.mult))
            dve.tensor_scalar(tab[:, 16:32], tab[:, 16:32], cst[0:E, C_EID:C_EID + 1], None, ALU.mult).then_inc(tab_ready, 1)

            def overflow_out():
                dve.wait_ge(tab_done, 1)
                step(dve.tensor_copy(offs, ps[:, DN, 0:16]))
                dve.tensor_copy(over_i[0:1, 0:17], ps[0:1, DN, 16:33]).then_inc(over_ready, 1)

            def pair(i, first=False, last=False):
                for side in range(2):
                    n = i * 2 + side
                    gate_part(n)
                    dve.wait_ge(pieces_used, n * 12 + 5)
                    if not (last and side):
                        select(n + 1)
                    if side == 0 and not first:
                        select_pair(i - 1)
                    up_part(n)
                    if side == 0 and first:
                        overflow_out()
                    if not (last and side):
                        gathered_out(n + 1)

            pair(0, first=True)
            with dve.Fori(1, E // 2 - 1) as i:
                pair(i)
            pair(E // 2 - 1, last=True)
            dve.wait_ge(sel_turned, E // 2 - 1)
            select_pair(E // 2 - 1)

            count = dve.value_load(over_i[0:1, 16:17], min_val=0, max_val=MAX_OVER)
            with dve.If(count > 0):
                with dve.Fori(0, count) as k:
                    n = k + E
                    e = dve.value_load(over_i[0:1, bass.ds(k, 1)], min_val=0, max_val=E - 1)
                    dve.wait_ge(sel_turned, k + E // 2)
                    dve.tensor_tensor(iota_o, iota, offs[:, bass.ds(k, 1)].broadcast_to([P, SLOTS]), ALU.add)\
                       .then_inc(fin_step, 1)
                    dve.wait_ge(fin_step, k + 1)
                    ids = iota_o.rearrange("p (a c) -> p a c", a=1).broadcast_to([P, NB, SLOTS])
                    select(e, ids)
                    select_p(n + 1, 0, e, ids).then_inc(selp_ready, 1)
                    gathered_out(n)
                    gate_part(n)
                    up_part(n)

            dve.wait_ge(combined, count + E // 2)
            dve.wait_ge(ld_gfin, 16)
            for b in range(NB):
                dve.tensor_tensor(xs[:, b, :], xs[:, b, :], ps[:, Y + 2 * b:Y + 2 * b + 2, :].rearrange("p a c -> p (a c)"),
                                  ALU.add).then_inc(res_ready, 1)
                dve.wait_ge(res_ready, 4 + b + 1)
                dve.tensor_tensor_reduce(work[:, 1536:2560], xs[:, b, :], xs[:, b, :], 1.0, 0.0, ALU.mult, ALU.add,
                                         stat[:, 4 + b:5 + b]).then_inc(sq_done, 1)
                dve.wait_ge(sq_done, 2 * NB + b + 1)
                variance(2 * NB + b)
            for b in range(NB):
                normalise(2 * NB + b, b)
                dve.wait_ge(xn_ready, 2 * NB + b + 1)
                dve.tensor_tensor(xn[:, b, :], xn[:, b, :], g_fin[:], ALU.mult).then_inc(fin_ready, 1)


_INS = ["x", "ln_mix_g", "w_in", "b_gate_a", "b_gate_b", "w_o_a", "w_o_b", "w_out", "ln_ffn_g", "w_router", "b_router",
        "w_gate", "b_gate", "w_up", "b_up", "w_down", "b_down", "ln_final_g"]


def kernel(**inputs):
    import numpy as _np
    import concourse.bacc as _bacc
    from concourse import mybir as _mybir
    from concourse.bass_utils import run_bass_kernel_spmd as _run

    nc = _bacc.Bacc("TRN2", target_bir_lowering=False, num_devices=1)
    arrays, args = {}, []
    given = {name: _np.ascontiguousarray(inputs[name]) for name in _INS}
    given["consts"], given["masks"] = shape_constants()
    for name, a in given.items():
        arrays[f"in_{name}_dram"] = a
        args.append(nc.dram_tensor(f"in_{name}_dram", a.shape, _mybir.dt.from_np(a.dtype), kind="ExternalInput").ap())
    out = nc.dram_tensor("out_dram", (1, SEQ, D), _mybir.dt.float32, kind="ExternalOutput").ap()
    layer(nc, *args, out)
    r = _run(nc, [arrays], core_ids=[0])
    return r.results[0]["out_dram"]
```

```python
from contextlib import ExitStack

import concourse.bass as bass
from concourse import mybir

P = 128
D = 1024
KT = D // P
SEQ = 256
NB = SEQ // P
HD = 64
HEADS_A = 8
HEADS_G = 4
DILATIONS = (1, 4, 16)
BAND = 128
NG = len(DILATIONS)
WIDTH_A = HEADS_A * HD
WIDTH_B = NG * HEADS_G * HD
ROT = 16
SCALE = HD ** -0.5
EPS = 1e-5
E = 32
TOP_K = 4
SLOTS = 64
MAX_OVER = SEQ * TOP_K // (SLOTS + 1)
PIECES = 12
HEAD = 7
AHEAD_PAIRS = 4
PARTS = 4
LIMIT = 7.0
ALPHA = 1.702
FAR = 4096.0
HIDE = -1.0e30

F32 = mybir.dt.float32
F32R = mybir.dt.float32r
I32 = mybir.dt.int32
U32 = mybir.dt.uint32
ALU = mybir.AluOpType
ACT = mybir.ActivationFunctionType
AX = mybir.AxisListType

CHUNK = 512
QK_CHUNKS = {0: 0, 1: 4, 3: 8, 4: 12, 5: 16}
V_CHUNKS = {2: (0, 512), 6: (512, 512), 7: (1024, 256)}
GATE_CHUNK0 = 8
N_CHUNKS = 12
CHUNK_COL = [0, 512, 1024, 1536, 2048, 2560, 3072, 3584, 3840, 4352, 4864, 5376]
QA, KA, QB, KB = 0, 4, 8, 14

C_ID, C_TRI, C_ONE, C_IOTA, C_EID, C_COS, C_SIN = 0, 128, 256, 384, 448, 449, 481
N_CONST = 513
MASK_A = [(0, 128), (128, 256)]
MASK_B = [(384, 384), (768, 768)]
N_MASK = 1536


def shape_constants():
    import numpy as np
    c = np.zeros((P, N_CONST), np.float32)
    row, col = np.arange(P)[:, None], np.arange(P)[None, :]
    c[:, C_ID:C_ID + P] = row == col
    c[:, C_TRI:C_TRI + P] = row < col
    c[:, C_ONE:C_ONE + P] = 1.0
    c[:, C_IOTA:C_IOTA + 64] = np.arange(64)
    c[:, C_EID] = np.arange(P)
    half = ROT // 2
    inv = np.float32(500000.0) ** (-np.arange(half, dtype=np.float32) / np.float32(half))
    for b in range(NB):
        ang = (np.arange(P) + P * b).astype(np.float32)[:, None] * inv.astype(np.float32)[None, :]
        cos, sin = np.cos(ang).astype(np.float32), np.sin(ang).astype(np.float32)
        c[:, C_COS + b * ROT:C_COS + (b + 1) * ROT] = np.concatenate([cos, cos], 1)
        c[:, C_SIN + b * ROT:C_SIN + (b + 1) * ROT] = np.concatenate([-sin, sin], 1)
    m = np.full((P, N_MASK), HIDE, np.float32)
    for b in range(NB):
        keys = P * (b + 1)
        back = (row + P * b) - np.arange(keys)[None, :]
        at = MASK_A[b][0]
        m[:, at:at + keys][back >= 0] = 0.0
        for g, dil in enumerate(DILATIONS):
            at = MASK_B[b][0] + g * keys
            m[:, at:at + keys][(back >= 0) & (back % dil == 0) & (back <= dil * BAND)] = 0.0
    return c, m


def layer(nc, x, ln_mix_g, w_in, b_gate_a, b_gate_b, w_o_a, w_o_b, w_out, ln_ffn_g, w_router, b_router,
          w_gate, b_gate, w_up, b_up, w_down, b_down, ln_final_g, consts, masks, out):
    ctx = ExitStack()

    def sb(name, shape, dt=F32):
        return ctx.enter_context(nc.sbuf_tensor(name, shape, dt))

    def sem(name):
        return ctx.enter_context(nc.semaphore(name))

    with ctx:
        wg_at = nc.sbuf_base + (-nc.sbuf_base) % 32
        wg = sb("wg", [P, KT, D])
        wu = sb("wu", [P, KT, D])
        wd = sb("wd", [P, KT, D])
        slots = [wu[:, 0:4, :], wu[:, 4:8, :], wd[:, 0:4, :], wd[:, 4:8, :]]
        slots = [s.rearrange("p a f -> p (a f)").rearrange("p (k c) -> p k c", c=CHUNK) for s in slots]
        w_hi = nc.alloc_sbuf_tensor_at("w_hi", [P, 2, KT, CHUNK], F32R, offset=wg_at)
        w_lo = nc.alloc_sbuf_tensor_at("w_lo", [P, 4, KT, CHUNK], F32R, offset=wg_at + KT * D * 4)
        woa = wu[:, 0:4, :]
        wob = wu[:, 4:6, :]
        wo_hi, wo_lo = [t[:, 0:2].rearrange("p s k c -> p (s k c)").rearrange("p (k n) -> p k n", n=D) for t in (w_hi, w_lo)]
        wo = wd

        xs = sb("xs", [P, NB, D])
        xn_at = nc.sbuf_base + (-nc.sbuf_base) % 32
        xn = sb("xn", [P, NB, D])
        h_t = sb("h_t", [P, KT, SEQ])
        h_lo = nc.alloc_sbuf_tensor_at("h_lo", [P, NB, KT, P], F32R, offset=xn_at)
        h_hi = nc.alloc_sbuf_tensor_at("h_hi", [P, NB, KT, P], F32R, offset=xn_at + NB * D * 4)
        o_hi, o_lo = [t[:].rearrange("p b k t -> p (b k t)").rearrange("p (k t) -> p k t", t=SEQ) for t in (h_hi, h_lo)]
        v_tok = sb("v_tok", [P, NB, 1280])
        attn = sb("attn", [P, 20 * SEQ + N_MASK])
        qk_t = attn[:, 0:20 * SEQ].rearrange("p (k t) -> p k t", t=SEQ)
        msk = attn[:, 20 * SEQ:20 * SEQ + N_MASK]
        mix_t = qk_t[:, 0:8, :]
        gates = sb("gates", [P, 2, KT, SEQ])
        o_t = sb("o_t", [P, 6, SEQ])
        work = sb("work", [P, 4608])
        stage = [work[:, 0:512], work[:, 512:1024]]
        rot_a = work[:, 1024:1152]
        rot_b = work[:, 1152:1280]
        probs = [work[:, 0:768], work[:, 768:1536]]
        masked = [work[:, 1536:2304], work[:, 2304:3072]]
        p_t = [work[:, 3072:3840], work[:, 3840:4608]]
        cst = sb("cst", [P, N_CONST])
        rows = sb("rows", [32, P])
        cols = sb("cols", [P, 32])
        bias_tab = sb("bias_tab", [P, D])
        b_dn = [v_tok[0:E, 1, 768:1280], msk[0:E, D:D + 512]]
        w_rt = sb("w_rt", [P, KT, E])
        b_rt = sb("b_rt", [P, E])
        g_fin = msk[:, 0:D]
        stat = sb("stat", [P, 64])
        second = [attn[:, 8 * SEQ:16 * SEQ], attn[:, 16 * SEQ:24 * SEQ],
                  v_tok[:].rearrange("p b c -> p (b c)")[:, 0:2 * D], work[:, 2560:2560 + 2 * D],
                  xn[:].rearrange("p b c -> p (b c)"), attn[:, 0:8 * SEQ], h_t[:].rearrange("p k t -> p (k t)")]
        second = [t.rearrange("p (k c) -> p k c", c=D) for t in second]

        def tile2k(g, k):
            return gates[:, g, k:k + 2, :].rearrange("p a t -> p (a t)")

        x_rows, g_act, sig, u_act, a_rows = tile2k(0, 0), tile2k(0, 2), tile2k(0, 4), tile2k(0, 6), tile2k(1, 0)
        x_g = tile2k(1, 2).rearrange("p (k c) -> p k c", c=SLOTS)
        y_pair = gates[:, 1, 4:8, :].rearrange("p a t -> p (a t)")
        a_t = o_t[:, 0:2, :].rearrange("p a t -> p (a t)").rearrange("p (k c) -> p k c", c=SLOTS)
        sel_t = o_t[:, 2, :]
        sel = work[:, 0:128].rearrange("p (b c) -> p b c", c=SLOTS)
        pick_bias = work[:, 128:256].rearrange("p (m c) -> p m c", c=SLOTS)
        sel_p = work[:, 1536:1792].rearrange("p (b c) -> p b c", c=2 * SLOTS)
        iota_o = work[:, 256:320]
        pick = [work[:, at:at + 128].rearrange("p (k e) -> p k e", e=E) for at in (384, 512)]
        pick_p = work[:, 640:768].rearrange("p (k e) -> p k e", e=E)
        logits = work[:, 768:832].rearrange("p (b e) -> p b e", e=E)
        chosen = work[:, 832:896].rearrange("p (b e) -> p b e", e=E)
        prob = work[:, 896:960].rearrange("p (b e) -> p b e", e=E)
        pos = work[:, 960:1024].rearrange("p (b e) -> p b e", e=E)
        prob_t = work[0:E, 1024:1280]
        tab = work[0:E, 1280:1344]
        offs = work[:, 1344:1360]
        top_v = work[:, 1400:1416]
        top_f = work[:, 1416:1424]
        top_e = work[:, 1424:1432]
        top_i = sb("top_i", [P, NB, 8], U32)
        over_i = sb("over_i", [1, 20], I32)

        ps = ctx.enter_context(nc.psum_tensor("ps", [P, 8, 512], F32))
        G, U, X, DN, Y = 0, 1, 2, 3, 4
        PROJ = ((0, 1), (4, 5))
        MIX = (0, 1, 6, 7)

        ident = cst[:, C_ID:C_ID + P]
        tri = cst[:, C_TRI:C_TRI + P]
        ones = cst[:, C_ONE:C_ONE + P]
        iota = cst[:, C_IOTA:C_IOTA + 64]

        ld_x = [sem(f"ld_x{b}") for b in range(NB)]
        ld_mix, ld_cst, ld_msk, ld_rows, ld_small = sem("ld_mix"), sem("ld_cst"), sem("ld_msk"), sem("ld_rows"), sem("ld_small")
        ld_first = [sem(f"ld_first{q}") for q in range(PARTS)]
        ld_chunk = [sem(f"ld_chunk{s}") for s in range(4)]
        ld_wo, ld_wout, ld_gfin, ld_bdn = sem("ld_wo"), sem("ld_wout"), sem("ld_gfin"), sem("ld_bdn")
        ld_main = [sem(f"ld_main{q}") for q in range(PIECES)]
        ld_second = [sem(f"ld_second{q}") for q in range(HEAD)]
        wo_used = sem("wo_used")
        o_hi_ready, o_lo_ready = sem("o_hi_ready"), sem("o_lo_ready")
        oproj_done, wout_done = sem("oproj_done"), sem("wout_done")
        sq_act = sem("sq_act")
        sq_done, var_ready, rstd_ready, xn_ready = sem("sq_done"), sem("var_ready"), sem("rstd_ready"), sem("xn_ready")
        neg_half = sem("neg_half")
        rows_turned, cols_ready = sem("rows_turned"), sem("cols_ready")
        x_turned, h_ready, h_lo_ready = sem("x_turned"), sem("h_ready"), sem("h_lo_ready")
        hi_ready, lo_ready = sem("hi_ready"), sem("lo_ready")
        proj_done, proj_read = sem("proj_done"), sem("proj_read")
        rot_step, rotated = sem("rot_step"), sem("rotated")
        qk_turned, qk_ready = sem("qk_turned"), sem("qk_ready")
        scored, soft_step, row_max, exp_done, probs_ready = sem("scored"), sem("soft_step"), sem("row_max"), sem("exp_done"), sem("probs_ready")
        p_turned, p_ready = sem("p_turned"), sem("p_ready")
        pv_done, o_ready = sem("pv_done"), sem("o_ready")
        gate_done, gate_read = sem("gate_done"), sem("gate_read")
        gates_ready = sem("gates_ready")
        mix_step, mix_ready = sem("mix_step"), sem("mix_ready")
        res_ready = sem("res_ready")
        bias_zero = sem("bias_zero")
        logit_done, rt_step = sem("logit_done"), sem("rt_step")
        rt_exp_in, rt_exp = sem("rt_exp_in"), sem("rt_exp")
        chosen_ready, prob_ready = sem("chosen_ready"), sem("prob_ready")
        pos_done, prob_turned, prob_t_ready = sem("pos_done"), sem("prob_turned"), sem("prob_t_ready")
        count_done, nov_ready, ostart_done, tab_ready, tab_done, over_ready = (
            sem("count_done"), sem("nov_ready"), sem("ostart_done"), sem("tab_ready"), sem("tab_done"), sem("over_ready"))
        pieces_used = sem("pieces_used")
        sel_ready, gathered, x_rows_ready = sem("sel_ready"), sem("gathered"), sem("x_rows_ready")
        xg_turned, xg_ready = sem("xg_turned"), sem("xg_ready")
        g_ready, sig_done, act_ready = sem("g_ready"), sem("sig_done"), sem("act_ready")
        sel_step, g_step, u_step, selp_step = sem("sel_step"), sem("g_step"), sem("u_step"), sem("selp_step")
        a_turned, a_t_ready, y_ready = sem("a_turned"), sem("a_t_ready"), sem("y_ready")
        selp_ready, sel_turned, sel_t_ready = sem("selp_ready"), sem("sel_turned"), sem("sel_t_ready")
        combined = sem("combined")
        fin_sum = sem("fin_sum")
        fin_step, fin_ready, stored = sem("fin_step"), sem("fin_ready"), sem("stored")

        x_v = x[0].rearrange("(b p) d -> b p d", p=P)
        out_v = out[0].rearrange("(b p) d -> b p d", p=P)
        win_v = w_in[0].rearrange("(k p) n -> p k n", p=P)
        row_v = [t[0].rearrange("(k p) -> k p", p=P) for t in (ln_mix_g, b_gate_a, b_gate_b, ln_ffn_g)]
        expert_v = [t[0].rearrange("e (k p) f -> e p k f", p=P) for t in (w_gate, w_up, w_down)]
        expert_sb = [wg, wu, wd]

        units = [("a", h, None) for h in range(HEADS_A)]
        units += [("b", 2 * q + j, b) for q in range(HEADS_G // 2) for b in range(NB) for j in range(2)]
        N_UNITS = len(units)

        def unit_rows(u):
            kind, h, b = units[u]
            if kind == "a":
                return [(0, 0, 128, MASK_A[0][0]), (1, 128, 256, MASK_A[1][0])]
            return [(b, 0, MASK_B[b][1], MASK_B[b][0])]

        def unit_blocks(u):
            kind, h, b = units[u]
            if kind == "a":
                return [(0, 0, 0, HD * h, True, True), (1, 128, 0, HD * h, True, False),
                        (1, 256, 1, HD * h, False, True)]
            last = NG * (b + 1) - 1
            return [(b, P * (g * (b + 1) + kb), kb, WIDTH_A + HD * (HEADS_G * g + h),
                     g == 0 and kb == 0, g * (b + 1) + kb == last) for g in range(NG) for kb in range(b + 1)]

        def unit_out(u):
            kind, h, b = units[u]
            return (h // 2 if kind == "a" else 4 + h // 2), h % 2

        def width(u):
            return len(unit_blocks(u)) * P

        def parts_after(u):
            return [(GATE_CHUNK0 + 1 + u // 4, q) for q in ((0,), (1,), (2, 3), ())[u % 4]]

        n_soft = [sum(len(unit_rows(v)) for v in range(u)) for u in range(N_UNITS + 1)]
        tile_end = [0, 1, 2, 3, 5, 7]

        block = ctx.enter_context(nc.Block())

        @block.sync
        def _(sp):
            sp.dma_start(xs[:, 0, :], x_v[0]).then_inc(ld_x[0], 16)

            def chunk(c):
                if c >= 4:
                    sp.wait_ge(proj_done, NB * (c - 3))
                n = V_CHUNKS[c][1] if c in V_CHUNKS else CHUNK
                sp.dma_start(slots[c % 4][:, :, 0:n], win_v[:, :, CHUNK_COL[c]:CHUNK_COL[c] + n])\
                  .then_inc(ld_chunk[c % 4], 16)

            def piece(q, e, side, first=0, step=1):
                m, k = q // 4, 2 * (q % 4)
                weights = expert_v[m][first:E:step][e, :, k:k + 2, :]
                if side and q < HEAD:
                    sp.dma_start(second[q], weights).then_inc(ld_second[q], 16)
                else:
                    sp.dma_start(expert_sb[m][:, k:k + 2, :], weights).then_inc(ld_main[q], 16)

            sp.dma_start(cst[:], consts).then_inc(ld_cst, 16)
            for q in range(PARTS):
                sp.dma_start(slots[0][:, 2 * q:2 * q + 2, :], win_v[:, 2 * q:2 * q + 2, 0:CHUNK]).then_inc(ld_first[q], 16)
            sp.dma_start(xs[:, 1, :], x_v[1]).then_inc(ld_x[1], 16)
            for c in range(1, 4):
                chunk(c)
            for r in range(1, 4):
                sp.dma_start(rows[8 * r:8 * r + 8, :], row_v[r]).then_inc(ld_rows, 16)
            chunk(4)
            sp.dma_start(msk, masks).then_inc(ld_msk, 16)
            sp.dma_start(bias_tab[0:E, :], b_gate[0]).then_inc(ld_small, 16)
            sp.dma_start(bias_tab[E:2 * E, :], b_up[0]).then_inc(ld_small, 16)
            sp.dma_start(w_rt[:], w_router[0].rearrange("(k p) e -> p k e", p=P)).then_inc(ld_small, 16)
            sp.dma_start(b_rt[:], b_router.broadcast_to([P, E])).then_inc(ld_small, 16)
            for c in range(5, N_CHUNKS):
                chunk(c)
            sp.wait_ge(gate_done, 8)
            sp.dma_start(woa, w_o_a[0].rearrange("(k p) n -> p k n", p=P)).then_inc(ld_wo, 16)
            sp.dma_start(wob, w_o_b[0].rearrange("(k p) n -> p k n", p=P)).then_inc(ld_wo, 16)
            piece(7, 0, 0)
            for h in range(2):
                sp.wait_ge(gate_done, 12 + 4 * h)
                sp.dma_start(wo[:, 4 * h:4 * h + 4, :], w_out[0].rearrange("(k p) n -> p k n", p=P)[:, 4 * h:4 * h + 4, :])\
                  .then_inc(ld_wout, 16)
            sp.wait_ge(scored, N_UNITS)
            piece(0, 1, 1)
            sp.wait_ge(row_max, n_soft[N_UNITS])
            piece(1, 1, 1)
            sp.wait_ge(pv_done, N_UNITS // 2)
            piece(2, 1, 1)
            piece(3, 1, 1)
            for h in range(2):
                sp.dma_start(b_dn[h], b_down[0][:, 512 * h:512 * h + 512]).then_inc(ld_bdn, 16)
            sp.wait_ge(oproj_done, KT)
            piece(4, 1, 1)
            for q in range(7):
                piece(q, 0, 0)
            for q in range(8, PIECES):
                sp.wait_ge(wo_used, q - 7)
                piece(q, 0, 0)
            piece(5, 1, 1)
            sp.wait_ge(logit_done, NB)
            piece(6, 1, 1)

            def head(i, item):
                for q in range(HEAD):
                    sp.wait_ge(pieces_used, i * (2 * PIECES) + ((item - 2) * PIECES + q + 1))
                    piece(q, i, item % 2, first=item, step=2)

            def tail(i, item):
                for q in range(HEAD, PIECES):
                    sp.wait_ge(pieces_used, i * (2 * PIECES) + ((item - 1) * PIECES + q + 1))
                    piece(q, i, item % 2, first=item, step=2)

            with sp.Fori(0, AHEAD_PAIRS) as i:
                head(i, 2)
                tail(i, 1)
                head(i, 3)
                tail(i, 2)
            tail(AHEAD_PAIRS, 1)
            with sp.Fori(AHEAD_PAIRS + 1, E // 2) as i:
                for item in range(2):
                    head(i, item)
                    tail(i, item)
            sp.wait_ge(pieces_used, (E - 1) * PIECES + HEAD)
            sp.dma_start(g_fin, ln_final_g.rearrange("(a d) -> a d", a=1).broadcast_to([P, D])).then_inc(ld_gfin, 16)

            sp.wait_ge(over_ready, 1)
            count = sp.value_load(over_i[0:1, 16:17], min_val=0, max_val=MAX_OVER)
            with sp.If(count > 0):
                with sp.Fori(0, count) as k:
                    e = sp.value_load(over_i[0:1, bass.ds(k, 1)], min_val=0, max_val=E - 1)
                    for q in range(PIECES):
                        sp.wait_ge(pieces_used, (k + E - 1) * PIECES + q + 1)
                        piece(q, e, 0)
            for b in range(NB):
                for h in range(2):
                    sp.wait_ge(fin_ready, 2 * b + h + 1)
                    sp.dma_start(out_v[b][:, 512 * h:512 * h + 512], xn[:, b, 512 * h:512 * h + 512]).then_inc(stored, 16)
            sp.wait_ge(stored, 32 * NB)

        @block.gpsimd
        def _(pool):
            pool.memset(bias_tab[2 * E:P, :], 0.0).then_inc(bias_zero, 1)
            pool.wait_ge(bias_zero, 1)
            pool.memset(stat[:, 60:62], -0.5).then_inc(neg_half, 1)
            pool.wait_ge(neg_half, 1)
            for n in range(3 * NB):
                pool.wait_ge(var_ready, n + 1)
                pool.tensor_tensor(stat[:, 12 + n:13 + n], stat[:, 6 + n:7 + n], stat[:, 60:61], ALU.pow)\
                    .then_inc(rstd_ready, 1)

        @block.scalar
        def _(act):
            act.dma_start(rows[0:8, :], row_v[0]).then_inc(ld_mix, 16)

            def split_hi(c, q):
                n = V_CHUNKS[c][1] if c in V_CHUNKS else CHUNK
                act.activation(w_hi[:, c % 2, 2 * q:2 * q + 2, 0:n], slots[c % 4][:, 2 * q:2 * q + 2, 0:n], ACT.Copy)\
                   .then_inc(hi_ready, 1)

            def chunk_loaded(c):
                if c == N_CHUNKS:
                    act.wait_ge(ld_wo, 32)
                else:
                    act.wait_ge(ld_chunk[c % 4], 16 * (c // 4 + (c % 4 > 0)))

            def split_hi_chunk(c):
                chunk_loaded(c)
                for q in range(PARTS):
                    split_hi(c, q)

            for q in range(PARTS):
                act.wait_ge(ld_first[q], 16)
                split_hi(0, q)
            act.wait_ge(ld_x[1], 16)
            act.activation(work[:, 1024:2048], xs[:, 1, :], ACT.Square, accum_out=stat[:, 1:2]).then_inc(sq_act, 1)
            split_hi_chunk(1)

            qk_seen = 0
            for c in range(8):
                for b in range(NB):
                    act.wait_ge(proj_done, NB * c + b + 1)
                    if c in QK_CHUNKS:
                        if qk_seen >= 2:
                            act.wait_ge(qk_turned, qk_seen - 1)
                        act.activation(stage[b], ps[:, PROJ[c % 2][b], :], ACT.Copy).then_inc(proj_read, 1)
                        qk_seen += 1
                    else:
                        at, n = V_CHUNKS[c]
                        act.activation(v_tok[:, b, at:at + n], ps[:, PROJ[c % 2][b], 0:n], ACT.Copy).then_inc(proj_read, 1)
                if c + 2 <= GATE_CHUNK0:
                    split_hi_chunk(c + 2)

            def evac_gate(t):
                act.wait_ge(gate_done, t + 1)
                act.activation(gates[:, t // 8, t % 8, :], ps[:, t % 2, 0:SEQ], ACT.Identity,
                               bias=cols[:, 8 + t:9 + t]).then_inc(gate_read, 1)

            def exps(u):
                for n, (b, at, w, _m) in enumerate(unit_rows(u)):
                    s = n_soft[u] + n
                    act.wait_ge(row_max, s + 1)
                    act.activation(probs[u % 2][:, at:at + w], masked[u % 2][:, at:at + w], ACT.Exp,
                                   bias=stat[:, 20 + (s % 4):21 + (s % 4)], scale=SCALE,
                                   accum_out=stat[:, 24 + (s % 4):25 + (s % 4)]).then_inc(exp_done, 1)

            def evac_o(t):
                act.wait_ge(pv_done, tile_end[t] + 1)
                act.activation(o_t[:, t, :], ps[:, 6 + t % 2, 0:SEQ], ACT.Copy).then_inc(o_ready, 1)

            act.wait_ge(cols_ready, 2)
            tiles_out = 0
            for u in range(N_UNITS):
                if u >= 2:
                    act.wait_ge(p_turned, u - 1)
                exps(u)
                evac_gate(u)
                for c, q in parts_after(u):
                    if q == 0:
                        chunk_loaded(c)
                        act.wait_ge(gate_done, 4 * (c - GATE_CHUNK0 - 1))
                    split_hi(c, q)
                while tiles_out < len(tile_end) and 2 * tile_end[tiles_out] + 2 <= u - 1:
                    evac_o(tiles_out)
                    tiles_out += 1
            def split_o(t0, t1):
                act.wait_ge(o_ready, t1)
                act.activation(o_hi[:, t0:t1, :], o_t[:, t0:t1, :], ACT.Copy).then_inc(o_hi_ready, 1)

            act.wait_ge(gate_done, 16)
            split_o(0, 5)
            split_hi(N_CHUNKS + 1, 0)
            split_hi(N_CHUNKS + 1, 1)
            evac_o(5)
            split_o(5, 6)
            act.wait_ge(gate_read, 16)
            for v in (gates[:, :, 0:2, :], gates[:, :, 2:KT, :]):
                act.activation(v, v, ACT.Sigmoid).then_inc(gates_ready, 1)

            for b in range(NB):
                act.wait_ge(rt_exp_in, b + 1)
                act.activation(top_e[:, 4 * b:4 * b + 4], top_v[:, 8 * b:8 * b + 4], ACT.Exp,
                               bias=stat[:, 30 + b:31 + b], accum_out=stat[:, 32 + b:33 + b]).then_inc(rt_exp, 1)

            def item_sigmoid(n):
                act.wait_ge(g_ready, n + 1)
                act.activation(sig, g_act, ACT.Sigmoid, scale=ALPHA).then_inc(sig_done, 1)

            def turned_selection(pairs, bank=DN):
                act.wait_ge(sel_turned, pairs)
                act.activation(sel_t, ps[:, bank, 0:SEQ], ACT.Copy).then_inc(sel_t_ready, 1)

            def gathered_out(n):
                act.wait_ge(gathered, n + 1)
                act.activation(x_rows, ps[:, X, :], ACT.Copy).then_inc(x_rows_ready, 1)

            def turned_activation(n):
                act.wait_ge(a_turned, n + 1)
                act.activation(a_t.rearrange("p (h j) c -> p j h c", h=2),
                               ps[:, G, :].rearrange("p (j h c) -> p j h c", h=2, c=SLOTS), ACT.Copy)\
                   .then_inc(a_t_ready, 1)

            def item_out(n, side):
                act.wait_ge(pieces_used, n * PIECES + 12)
                for h in range(2):
                    act.activation(y_pair[SLOTS * side:SLOTS * side + SLOTS, 512 * h:512 * h + 512],
                                   ps[SLOTS * h:SLOTS * h + SLOTS, DN, :], ACT.Copy).then_inc(y_ready, 1)

            def pair(i, first=False, last=False):
                for side in range(2):
                    n = i * 2 + side
                    item_sigmoid(n)
                    if not (last and side):
                        gathered_out(n + 1)
                    if side == 0 and not first:
                        turned_selection(i)
                    if last and side:
                        turned_selection(E // 2, bank=X)
                    turned_activation(n)
                    item_out(n, side)

            gathered_out(0)
            act.wait_ge(prob_turned, 1)
            act.activation(prob_t, ps[0:E, DN, 0:SEQ], ACT.Copy).then_inc(prob_t_ready, 1)
            pair(0, first=True)
            with act.Fori(1, E // 2 - 1) as i:
                pair(i)
            pair(E // 2 - 1, last=True)
            act.wait_ge(over_ready, 1)
            count = act.value_load(over_i[0:1, 16:17], min_val=0, max_val=MAX_OVER)
            with act.If(count > 0):
                with act.Fori(0, count) as k:
                    n = k + E
                    gathered_out(n)
                    item_sigmoid(n)
                    turned_activation(n)
                    item_out(n, 0)
                    turned_selection(k + (E // 2 + 1))
            for b in range(NB):
                for h in range(2):
                    n = 2 * b + h
                    act.wait_ge(res_ready, 4 + n + 1)
                    act.activation(work[:, 512 * n:512 * n + 512], xs[:, b, 512 * h:512 * h + 512], ACT.Square,
                                   accum_out=stat[:, 50 + n:51 + n]).then_inc(sq_act, 1)

        @block.tensor
        def _(pe):
            def turn(out_ap, in_ap):
                n = in_ap.shape[0]
                return pe.transpose(out_ap, in_ap, ident[0:n, 0:n])

            pe.wait_ge(ld_cst, 16)
            pe.wait_ge(ld_mix, 16)
            turn(ps[:, 6, 0:8], rows[0:8, :]).then_inc(rows_turned, 1)
            def turn_input(b):
                pe.wait_ge(xn_ready, b + 1)
                for h in range(2):
                    for k in range(4):
                        mm = turn(ps[:, 2 + 2 * b + h, P * k:P * k + P], xn[:, b, P * (4 * h + k):P * (4 * h + k) + P])
                    mm.then_inc(x_turned, 1)

            qk_turns = 0

            def turn_qk(c):
                nonlocal qk_turns
                for b in range(NB):
                    pe.wait_ge(rotated, qk_turns + 1)
                    if qk_turns >= 2:
                        pe.wait_ge(qk_ready, qk_turns - 1)
                    for k in range(4):
                        mm = turn(ps[:, 2 + b, P * k:P * k + P], stage[b][:, P * k:P * k + P])
                    mm.then_inc(qk_turned, 1)
                    qk_turns += 1

            def lo_by_hi(c, b, bank, n, last=False):
                pe.wait_ge(h_lo_ready, 2 * (b + 1))
                for k in range(KT):
                    mm = pe.matmul(ps[:, bank, 0:n], h_lo[:, b, k, :], w_hi[:, c % 2, k, 0:n],
                                   start=False, stop=(last and k == KT - 1))
                return mm

            def hi_by_lo(c, b, bank, n, last=False):
                for k in range(KT):
                    if k % 2 == 0:
                        pe.wait_ge(lo_ready, PARTS * c + k // 2 + 1)
                    mm = pe.matmul(ps[:, bank, 0:n], h_hi[:, b, k, :], w_lo[:, c % 4, k, 0:n],
                                   start=False, stop=(last and k == KT - 1))
                return mm

            for c in range(8):
                if c == 7:
                    pe.wait_ge(ld_rows, 48)
                    pe.wait_ge(cols_ready, 1)
                    turn(ps[:, 7, 0:32], rows[:]).then_inc(rows_turned, 1)
                n = V_CHUNKS[c][1] if c in V_CHUNKS else CHUNK
                for b in range(NB):
                    bank = PROJ[c % 2][b]
                    if c == 0 and b == 0:
                        turn_input(0)
                    if c >= 2:
                        pe.wait_ge(proj_read, NB * (c - 2) + b + 1)
                    for k in range(KT):
                        if k % 4 == 0:
                            pe.wait_ge(h_ready, 2 * b + k // 4 + 1)
                        if k % 2 == 0:
                            pe.wait_ge(hi_ready, PARTS * c + k // 2 + 1)
                        pe.matmul(ps[:, bank, 0:n], h_hi[:, b, k, :], w_hi[:, c % 2, k, 0:n], start=(k == 0), stop=False)
                    if b == 0:
                        lo_by_hi(c, b, bank, n)
                        if c == 0:
                            turn_input(1)
                        mm = hi_by_lo(c, b, bank, n, last=True)
                    else:
                        hi_by_lo(c, b, bank, n)
                        mm = lo_by_hi(c, b, bank, n, last=True)
                    mm.then_inc(proj_done, 1)
                if c >= 1 and (c - 1) in QK_CHUNKS:
                    turn_qk(c - 1)

            def scores(u):
                kind, h, b = units[u]
                base = 2 + 2 * (u % 2)
                if u >= 2:
                    pe.wait_ge(p_ready, u - 1)
                elif u == 1:
                    pe.wait_ge(proj_read, NB * 8)
                if kind == "a":
                    r = HD * (h % 2)
                    q, k = qk_t[r:r + HD, QA + h // 2, :], qk_t[r:r + HD, KA + h // 2, :]
                    pe.matmul(ps[:, base, 0:128], q[:, 0:128], k[:, 0:128], start=True, stop=True)
                    mm = pe.matmul(ps[:, base, 128:384], q[:, 128:256], k[:, 0:256], start=True, stop=True)
                else:
                    keys = P * (b + 1)
                    for g in range(NG):
                        hh = HEADS_G * g + h
                        r = HD * (hh % 2)
                        q, k = qk_t[r:r + HD, QB + hh // 2, :], qk_t[r:r + HD, KB + hh // 2, :]
                        at = g * keys
                        mm = pe.matmul(ps[:, base + at // 512, at % 512:at % 512 + keys], q[:, P * b:P * b + P],
                                       k[:, 0:keys], start=True, stop=True)
                mm.then_inc(scored, 1)

            def gate_tile(t):
                c = GATE_CHUNK0 + t // 4
                if t % 4 == 0:
                    pe.wait_ge(hi_ready, PARTS * (c + 1))
                    pe.wait_ge(lo_ready, PARTS * (c + 1))
                if t >= 2:
                    pe.wait_ge(gate_read, t - 1)
                elif t == 0:
                    pe.wait_ge(proj_read, NB * 7)
                cut = slice(P * (t % 4), P * (t % 4) + P)
                for k in range(KT):
                    pe.matmul(ps[:, t % 2, 0:SEQ], w_hi[:, c % 2, k, cut], h_hi[:, :, k, :], start=(k == 0), stop=False)
                    pe.matmul(ps[:, t % 2, 0:SEQ], w_hi[:, c % 2, k, cut], h_lo[:, :, k, :], start=False, stop=False)
                    mm = pe.matmul(ps[:, t % 2, 0:SEQ], w_lo[:, c % 4, k, cut], h_hi[:, :, k, :],
                                   start=False, stop=(k == KT - 1))
                mm.then_inc(gate_done, 1)

            def turn_probs(u):
                base = 2 + 2 * (u % 2)
                pe.wait_ge(probs_ready, n_soft[u + 1])
                for (_b, at, _k, _v, _f, _l) in unit_blocks(u):
                    mm = turn(ps[:, base + at // 512, at % 512:at % 512 + P], probs[u % 2][:, at:at + P])
                mm.then_inc(p_turned, 1)

            def weigh_values(q):
                t = unit_out(2 * q)[0]
                pe.wait_ge(p_ready, 2 * q + 2)
                if t >= 2:
                    pe.wait_ge(o_ready, t - 1)
                for n in range(len(unit_blocks(2 * q))):
                    for u in (2 * q, 2 * q + 1):
                        (b, at, kb, v, first, last) = unit_blocks(u)[n]
                        half = unit_out(u)[1]
                        mm = pe.matmul(ps[HD * half:HD * half + HD, 6 + t % 2, P * b:P * b + P],
                                       v_tok[:, kb, v:v + HD], p_t[u % 2][:, at:at + P], start=first, stop=last,
                                       skip_group_check=True)
                mm.then_inc(pv_done, 1)

            pe.wait_ge(qk_ready, 10)
            pe.wait_ge(cols_ready, 2)
            scores(0)
            for u in range(N_UNITS):
                gate_tile(u)
                if u + 1 < N_UNITS:
                    scores(u + 1)
                turn_probs(u)
                if u >= 2 and u % 2 == 0:
                    weigh_values(u // 2 - 1)
            weigh_values(N_UNITS // 2 - 1)

            def mixer_product(m, tiles, columns):
                for k in tiles:
                    pe.matmul(ps[:, MIX[m % 4], columns], wo_hi[:, k, P * m:P * m + P], o_hi[:, k, :],
                              start=(k == tiles[0]), stop=False)
                    pe.matmul(ps[:, MIX[m % 4], columns], wo_hi[:, k, P * m:P * m + P], o_lo[:, k, :], start=False, stop=False)
                    mm = pe.matmul(ps[:, MIX[m % 4], columns], wo_lo[:, k, P * m:P * m + P], o_hi[:, k, :],
                                   start=False, stop=(k == tiles[-1]))
                return mm

            def mixer_a(m):
                if m < 2:
                    pe.wait_ge(gate_read, 15 + m)
                elif m >= 4:
                    pe.wait_ge(mix_ready, m - 3)
                mixer_product(m, range(0, 4), slice(0, SEQ))

            pe.wait_ge(lo_ready, PARTS * (N_CHUNKS + 1))
            pe.wait_ge(o_lo_ready, 1)
            mixer_a(0)
            for m in range(KT):
                if m == 1:
                    pe.wait_ge(o_ready, 6)
                if m + 1 < KT:
                    mixer_a(m + 1)
                if m == 0:
                    pe.wait_ge(lo_ready, PARTS * (N_CHUNKS + 1) + 2)
                    pe.wait_ge(o_lo_ready, 2)
                mixer_product(m, range(4, 6), slice(SEQ, 2 * SEQ)).then_inc(oproj_done, 1)
            pe.wait_ge(ld_wout, 32)

            def out_product(b, h, ks=range(KT)):
                for k in ks:
                    if b == 0 and h == 0:
                        pe.wait_ge(mix_ready, k + 1)
                    mm = pe.matmul(ps[:, 2 + 2 * b + h, :], mix_t[:, k, P * b:P * b + P],
                                   wo[:, k, 512 * h:512 * h + 512], start=(k == 0), stop=(k == KT - 1))
                    if (b, h) == (1, 1) and k % 2:
                        mm.then_inc(wo_used, 1)
                if k == KT - 1 and (b, h) != (1, 1):
                    mm.then_inc(wout_done, 1)

            def turn_residual(b, h):
                pe.wait_ge(res_ready, 2 * b + h + 1)
                if b == 1:
                    pe.wait_ge(h_ready, 4 + h + 1)
                for k in range(4):
                    mm = turn(ps[:, 6 + h, P * k:P * k + P], xs[:, b, P * (4 * h + k):P * (4 * h + k) + P])
                mm.then_inc(x_turned, 1)

            def logits_of(b, ks=range(KT)):
                for k in ks:
                    if k % 4 == 0:
                        pe.wait_ge(h_ready, 4 + 2 * b + k // 4 + 1)
                    mm = pe.matmul(ps[:, b, 0:E], h_t[:, k, P * b:P * b + P], w_rt[:, k, :],
                                   start=(k == 0), stop=(k == KT - 1))
                if k == KT - 1:
                    mm.then_inc(logit_done, 1)

            out_product(0, 0)
            out_product(0, 1)
            out_product(1, 0)
            pe.wait_ge(ld_small, 16 * 4)
            pe.wait_ge(bias_zero, 1)
            turn_residual(0, 0)
            turn_residual(0, 1)
            out_product(1, 1, range(0, 4))
            turn_residual(1, 0)
            out_product(1, 1, range(4, KT))
            logits_of(0, range(0, 4))
            turn_residual(1, 1)
            logits_of(0, range(4, KT))
            logits_of(1)
            pe.wait_ge(chosen_ready, 1)
            pe.matmul(ps[:, X, 0:E], tri, chosen[:, 0, :], start=True, stop=True)
            pe.matmul(ps[:, X, E:2 * E], ones, chosen[:, 0, :], start=True, stop=False)
            pe.wait_ge(chosen_ready, 2)
            pe.matmul(ps[:, X, E:2 * E], tri, chosen[:, 1, :], start=False, stop=True).then_inc(pos_done, 1)
            for b in range(NB):
                mm = pe.matmul(ps[0:E, G, 0:1], chosen[:, b, :], ones[:, 0:1], start=(b == 0), stop=(b == NB - 1))
            mm.then_inc(count_done, 1)

            def gather(n):
                pe.wait_ge(sel_ready, n + 1)
                for b in range(NB):
                    for h in range(2):
                        mm = pe.matmul(ps[SLOTS * h:SLOTS * h + SLOTS, X, :], sel[:, b, :],
                                       xs[:, b, 512 * h:512 * h + 512], start=(b == 0), stop=(b == NB - 1),
                                       skip_group_check=True)
                mm.then_inc(gathered, 1)

            def turn_rows(bank, rows_ap):
                for j in range(4):
                    mm = turn(ps[:, bank, P * j:P * j + P], rows_ap[:, P * j:P * j + P])
                return mm

            def turn_gathered(n):
                pe.wait_ge(x_rows_ready, n + 1)
                turn_rows(X, x_rows).then_inc(xg_turned, 1)

            def turn_activation(n):
                pe.wait_ge(act_ready, n + 1)
                turn_rows(G, a_rows).then_inc(a_turned, 1)

            def product(m, heads, tails, side, bank, lhs, bias=True):
                if bias:
                    for h in range(2):
                        pe.matmul(ps[SLOTS * h:SLOTS * h + SLOTS, bank, :], pick_bias[:, m, :],
                                  bias_tab[:, 512 * h:512 * h + 512], start=True, stop=False, skip_group_check=True)
                for j in range(4):
                    q = 4 * m + j
                    if q < HEAD and side:
                        pe.wait_ge(ld_second[q], heads * 16)
                        w = second[q]
                    else:
                        pe.wait_ge(ld_main[q], (heads if q < HEAD else tails) * 16)
                        w = expert_sb[m][:, 2 * j:2 * j + 2, :]
                    for k in (2 * j, 2 * j + 1):
                        for h in range(2):
                            mm = pe.matmul(ps[SLOTS * h:SLOTS * h + SLOTS, bank, :], lhs[:, k, :],
                                           w[:, k - 2 * j, 512 * h:512 * h + 512],
                                           start=(k == 0 and not bias), stop=(k == KT - 1), skip_group_check=True)
                    mm.then_inc(pieces_used, 1)

            def gate_and_up(n, heads, side):
                pe.wait_ge(xg_ready, n + 1)
                product(0, heads, n + 1, side, G, x_g)
                product(1, heads, n + 1, side, U, x_g)

            def down(n, heads, side):
                product(2, heads, n + 1, side, DN, a_t, bias=False)

            def turn_selection(pairs, outputs, bank=DN):
                if bank == DN:
                    pe.wait_ge(y_ready, outputs)
                pe.wait_ge(selp_ready, pairs)
                for b in range(NB):
                    mm = turn(ps[:, bank, P * b:P * b + P], sel_p[:, b, :])
                mm.then_inc(sel_turned, 1)

            def combine(pairs, slots):
                pe.wait_ge(sel_t_ready, pairs)
                for b in range(NB):
                    for h in range(2):
                        mm = pe.matmul(ps[:, Y + 2 * b + h, :], sel_t[0:slots, P * b:P * b + P],
                                       y_pair[0:slots, 512 * h:512 * h + 512], start=False, stop=False,
                                       skip_group_check=True)
                        mm.then_inc(combined, 1)

            gather(0)
            pe.wait_ge(prob_ready, 2)
            for b in range(NB):
                mm = turn(ps[0:E, DN, P * b:P * b + P], prob[:, b, :])
            mm.then_inc(prob_turned, 1)
            turn_gathered(0)
            pe.wait_ge(nov_ready, 1)
            pe.wait_ge(prob_t_ready, 1)
            pe.matmul(ps[0:E, DN, 0:1], tri[0:E, 0:E], tab[:, 32:33], start=True, stop=True).then_inc(ostart_done, 1)

            def pair(i, first=False, last=False):
                for side in range(2):
                    n = i * 2 + side
                    gate_and_up(n, i + 1, side)
                    if not (last and side):
                        gather(n + 1)
                    if side == 0 and first:
                        pe.wait_ge(tab_ready, 1)
                        pe.matmul(ps[:, DN, 0:33], ones[0:E, :], tab[:, 0:33], start=True, stop=True).then_inc(tab_done, 1)
                    elif side == 0:
                        turn_selection(i, i * 4)
                        combine(i, P)
                    if not (last and side):
                        turn_gathered(n + 1)
                    else:
                        turn_selection(E // 2, 2 * E, bank=X)
                    turn_activation(n)
                    if side == 0 and first:
                        pe.wait_ge(over_ready, 1)
                    elif side == 1:
                        pe.wait_ge(y_ready, i * 4 + 2)
                    pe.wait_ge(a_t_ready, n + 1)
                    down(n, i + 1, side)
                    if side == 0 and first:
                        pe.wait_ge(ld_bdn, 32)
                        for b in range(NB):
                            for h in range(2):
                                pe.matmul(ps[:, Y + 2 * b + h, :], prob_t[:, P * b:P * b + P],
                                          b_dn[h], start=True, stop=False, skip_group_check=True)

            pair(0, first=True)
            with pe.Fori(1, E // 2 - 1) as i:
                pair(i)
            pair(E // 2 - 1, last=True)
            pe.wait_ge(y_ready, 2 * E)
            combine(E // 2, P)

            count = pe.value_load(over_i[0:1, 16:17], min_val=0, max_val=MAX_OVER)
            with pe.If(count > 0):
                with pe.Fori(0, count) as k:
                    n = k + E
                    gather(n)
                    turn_gathered(n)
                    gate_and_up(n, k + (E // 2 + 1), 0)
                    turn_activation(n)
                    pe.wait_ge(a_t_ready, n + 1)
                    down(n, k + (E // 2 + 1), 0)
                    turn_selection(k + (E // 2 + 1), n * 2 + 2)
                    combine(k + (E // 2 + 1), SLOTS)

        @block.vector
        def _(dve):
            def variance(n):
                dve.tensor_scalar(stat[:, 6 + n:7 + n], stat[:, n:n + 1], 1.0 / D, EPS, ALU.mult, ALU.add)\
                   .then_inc(var_ready, 1)

            def normalise(n, b):
                dve.wait_ge(rstd_ready, n + 1)
                dve.tensor_scalar(xn[:, b, :], xs[:, b, :], stat[:, 12 + n:13 + n], None, ALU.mult)\
                   .then_inc(xn_ready, 1)

            dve.wait_ge(ld_x[0], 16)
            dve.tensor_tensor_reduce(work[:, 0:1024], xs[:, 0, :], xs[:, 0, :], 1.0, 0.0, ALU.mult, ALU.add,
                                     stat[:, 0:1]).then_inc(sq_done, 1)
            dve.wait_ge(sq_done, 1)
            variance(0)
            normalise(0, 0)
            dve.wait_ge(rows_turned, 1)
            dve.tensor_copy(cols[:, 0:8], ps[:, 6, 0:8]).then_inc(cols_ready, 1)
            dve.wait_ge(cols_ready, 1)

            def spread(col, n):
                return col.rearrange("p (k a) -> p k a", a=1).broadcast_to([P, n[0], n[1]])

            def input_out(b):
                for h in range(2):
                    dve.wait_ge(x_turned, 2 * b + h + 1)
                    dve.tensor_tensor(h_hi[:, b, 4 * h:4 * h + 4, :],
                                      ps[:, 2 + 2 * b + h, :].rearrange("p (k t) -> p k t", t=P),
                                      spread(cols[:, 4 * h:4 * h + 4], (4, P)), ALU.mult).then_inc(h_ready, 1)
                for h in range(2):
                    dve.wait_ge(h_ready, 2 * b + h + 1)
                    for k in range(4 * h, 4 * h + 4):
                        ins = dve.scalar_tensor_tensor(h_lo[:, b, k, :], ps[:, 2 + 2 * b + h, P * (k % 4):P * (k % 4) + P],
                                                       cols[:, k:k + 1], h_hi[:, b, k, :], ALU.mult, ALU.subtract)
                    ins.then_inc(h_lo_ready, 1)

            def split_lo(c, q):
                n = V_CHUNKS[c][1] if c in V_CHUNKS else CHUNK
                dve.wait_ge(hi_ready, PARTS * c + q + 1)
                dve.tensor_tensor(w_lo[:, c % 4, 2 * q:2 * q + 2, 0:n], slots[c % 4][:, 2 * q:2 * q + 2, 0:n],
                                  w_hi[:, c % 2, 2 * q:2 * q + 2, 0:n], ALU.subtract).then_inc(lo_ready, 1)

            input_out(0)
            split_lo(0, 0)
            dve.wait_ge(sq_act, 1)
            variance(1)
            split_lo(0, 1)
            normalise(1, 1)
            split_lo(0, 2)
            split_lo(0, 3)
            input_out(1)

            steps = 0
            seen = 0
            turned_out = 0

            def qk_out(c):
                nonlocal turned_out
                t0 = QK_CHUNKS[c]
                for b in range(NB):
                    dve.wait_ge(qk_turned, turned_out + 1)
                    dve.tensor_copy(qk_t[:, t0:t0 + 4, P * b:P * b + P],
                                    ps[:, 2 + b, :].rearrange("p (k t) -> p k t", t=P)).then_inc(qk_ready, 1)
                    turned_out += 1

            for c in range(8):
                for q in range(PARTS):
                    split_lo(c + 1, q)
                if c == 7:
                    dve.wait_ge(rows_turned, 2)
                    dve.tensor_copy(cols[:], ps[:, 7, 0:32]).then_inc(cols_ready, 1)
                if c in QK_CHUNKS:
                    for b in range(NB):
                        dve.wait_ge(proj_read, NB * c + b + 1)
                        s = stage[b].rearrange("p (h d) -> p h d", d=HD)
                        ra = rot_a.rearrange("p (h d) -> p h d", d=ROT)
                        rb = rot_b.rearrange("p (h d) -> p h d", d=ROT)
                        cos = cst[:, C_COS + ROT * b:C_COS + ROT * b + ROT].rearrange("p (a d) -> p a d", a=1)
                        sin = cst[:, C_SIN + ROT * b:C_SIN + ROT * b + ROT].rearrange("p (a d) -> p a d", a=1)
                        if steps:
                            dve.wait_ge(rotated, seen)
                        dve.tensor_tensor(ra, s[:, :, 0:ROT], cos.broadcast_to([P, 8, ROT]), ALU.mult).then_inc(rot_step, 1)
                        dve.tensor_tensor(rb[:, :, 0:8], s[:, :, 8:16], sin[:, :, 0:8].broadcast_to([P, 8, 8]), ALU.mult)\
                           .then_inc(rot_step, 1)
                        dve.tensor_tensor(rb[:, :, 8:16], s[:, :, 0:8], sin[:, :, 8:16].broadcast_to([P, 8, 8]), ALU.mult)\
                           .then_inc(rot_step, 1)
                        steps += 3
                        dve.wait_ge(rot_step, steps)
                        dve.tensor_tensor(s[:, :, 0:ROT], ra, rb, ALU.add).then_inc(rotated, 1)
                        seen += 1
                if c >= 1 and (c - 1) in QK_CHUNKS:
                    qk_out(c - 1)

            dve.wait_ge(ld_msk, 16)
            dve.wait_ge(qk_turned, 10)
            soft_steps = 0

            def row_maxima(u):
                nonlocal soft_steps
                base = 2 + 2 * (u % 2)
                flat = ps[:, base:base + 2, :].rearrange("p a c -> p (a c)")
                dve.wait_ge(scored, u + 1)
                if u >= 2:
                    dve.wait_ge(exp_done, n_soft[u - 1])
                for n, (b, at, w, mk) in enumerate(unit_rows(u)):
                    s = n_soft[u] + n
                    dve.tensor_tensor_reduce(masked[u % 2][:, at:at + w], flat[:, at:at + w], msk[:, mk:mk + w],
                                             1.0, HIDE, ALU.add, ALU.max, stat[:, 28 + n:29 + n]).then_inc(soft_step, 1)
                    soft_steps += 1
                    dve.wait_ge(soft_step, soft_steps)
                    if s >= 4:
                        dve.wait_ge(exp_done, s - 3)
                    dve.tensor_scalar(stat[:, 20 + (s % 4):21 + (s % 4)], stat[:, 28 + n:29 + n], -SCALE, None, ALU.mult)\
                       .then_inc(row_max, 1)

            def divide(u):
                nonlocal soft_steps
                for n, (b, at, w, _m) in enumerate(unit_rows(u)):
                    s = n_soft[u] + n
                    dve.wait_ge(exp_done, s + 1)
                    dve.reciprocal(stat[:, 34 + (s % 4):35 + (s % 4)], stat[:, 24 + (s % 4):25 + (s % 4)]).then_inc(soft_step, 1)
                    soft_steps += 1
                    dve.wait_ge(soft_step, soft_steps)
                    pr = probs[u % 2][:, at:at + w]
                    dve.tensor_scalar(pr, pr, stat[:, 34 + (s % 4):35 + (s % 4)], None, ALU.mult).then_inc(probs_ready, 1)

            def probs_out(u):
                base = 2 + 2 * (u % 2)
                w = width(u)
                dve.wait_ge(p_turned, u + 1)
                if u >= 2:
                    dve.wait_ge(pv_done, u // 2)
                dve.tensor_copy(p_t[u % 2][:, 0:w], ps[:, base:base + 2, :].rearrange("p a c -> p (a c)")[:, 0:w])\
                   .then_inc(p_ready, 1)

            row_maxima(0)
            for u in range(N_UNITS):
                divide(u)
                if u + 1 < N_UNITS:
                    row_maxima(u + 1)
                for c, q in parts_after(u):
                    split_lo(c, q)
                probs_out(u)

            def split_o(n, t0, t1):
                dve.wait_ge(o_hi_ready, n)
                dve.tensor_tensor(o_lo[:, t0:t1, :], o_t[:, t0:t1, :], o_hi[:, t0:t1, :], ALU.subtract)\
                   .then_inc(o_lo_ready, 1)

            dve.wait_ge(gate_done, 16)
            split_o(1, 0, 5)
            split_lo(N_CHUNKS + 1, 0)
            split_lo(N_CHUNKS + 1, 1)
            split_o(2, 5, 6)

            for m in range(KT):
                dve.wait_ge(gates_ready, 1 if m < 2 else 2)
                dve.wait_ge(oproj_done, m + 1)
                ta, tb = work[:, 512 * (m % 2):512 * (m % 2) + 256], work[:, 512 * (m % 2) + 256:512 * (m % 2) + 512]
                dve.tensor_tensor(ta, ps[:, MIX[m % 4], 0:SEQ], gates[:, 0, m, :], ALU.mult).then_inc(mix_step, 1)
                dve.tensor_tensor(tb, ps[:, MIX[m % 4], SEQ:2 * SEQ], gates[:, 1, m, :], ALU.mult).then_inc(mix_step, 1)
                dve.wait_ge(mix_step, 2 * m + 2)
                dve.tensor_tensor(mix_t[:, m, :], ta, tb, ALU.add).then_inc(mix_ready, 1)
            dve.wait_ge(mix_ready, KT)

            rt = 0

            def step(ins):
                nonlocal rt
                rt += 1
                ins.then_inc(rt_step, 1)
                dve.wait_ge(rt_step, rt)

            def residual(b, h):
                q = slice(512 * h, 512 * h + 512)
                if (b, h) == (1, 1):
                    dve.wait_ge(wo_used, KT // 2)
                else:
                    dve.wait_ge(wout_done, 2 * b + h + 1)
                dve.tensor_tensor(xs[:, b, q], xs[:, b, q], ps[:, 2 + 2 * b + h, :], ALU.add).then_inc(res_ready, 1)
                dve.wait_ge(res_ready, 2 * b + h + 1)

            def squares(b, h):
                q = slice(512 * h, 512 * h + 512)
                step(dve.tensor_tensor_reduce(work[:, 1536 + 512 * h:2048 + 512 * h], xs[:, b, q], xs[:, b, q], 1.0, 0.0,
                                              ALU.mult, ALU.add, stat[:, 44 + 2 * b + h:45 + 2 * b + h]))

            def residual_norm(b):
                step(dve.tensor_tensor(stat[:, 2 + b:3 + b], stat[:, 44 + 2 * b:45 + 2 * b],
                                       stat[:, 45 + 2 * b:46 + 2 * b], ALU.add))
                variance(NB + b)

            def turned_residual(b, h):
                dve.wait_ge(x_turned, 4 + 2 * b + h + 1)
                dve.tensor_tensor(h_t[:, 4 * h:4 * h + 4, P * b:P * b + P],
                                  ps[:, 6 + h, :].rearrange("p (k t) -> p k t", t=P),
                                  spread(cols[:, 24 + 4 * h:24 + 4 * h + 4], (4, P)), ALU.mult).then_inc(h_ready, 1)

            def choose(b):
                dve.wait_ge(logit_done, b + 1)
                dve.wait_ge(rstd_ready, NB + b + 1)
                lg, tv = logits[:, b, :], top_v[:, 8 * b:8 * b + 8]
                step(dve.scalar_tensor_tensor(lg, ps[:, b, 0:E], stat[:, 14 + b:15 + b], b_rt[:], ALU.mult, ALU.add))
                step(dve.max(tv, lg))
                dve.tensor_scalar(stat[:, 30 + b:31 + b], tv[:, 0:1], -1.0, None, ALU.mult).then_inc(rt_exp_in, 1)
                step(dve.max_index(top_i[:, b, :], tv, lg))
                step(dve.tensor_copy(top_f[:, 4 * b:4 * b + 4], top_i[:, b, 0:4]))
                step(dve.tensor_tensor(pick[b], iota[:, 0:E].rearrange("p (a e) -> p a e", a=1).broadcast_to([P, TOP_K, E]),
                                       spread(top_f[:, 4 * b:4 * b + 4], (TOP_K, E)), ALU.is_equal))
                dve.tensor_reduce(chosen[:, b, :], pick[b].rearrange("p k e -> p e k"), AX.X, ALU.add).then_inc(chosen_ready, 1)

            def weigh(b):
                dve.wait_ge(rt_exp, b + 1)
                step(dve.reciprocal(stat[:, 40 + b:41 + b], stat[:, 32 + b:33 + b]))
                step(dve.tensor_scalar(top_e[:, 4 * b:4 * b + 4], top_e[:, 4 * b:4 * b + 4], stat[:, 40 + b:41 + b], None, ALU.mult))
                if b:
                    dve.wait_ge(prob_ready, b)
                step(dve.tensor_tensor(pick_p, pick[b], spread(top_e[:, 4 * b:4 * b + 4], (TOP_K, E)), ALU.mult))
                dve.tensor_reduce(prob[:, b, :], pick_p.rearrange("p k e -> p e k"), AX.X, ALU.add).then_inc(prob_ready, 1)

            residual(0, 0)
            squares(0, 0)
            residual(0, 1)
            squares(0, 1)
            residual_norm(0)
            residual(1, 0)
            turned_residual(0, 0)
            turned_residual(0, 1)
            squares(1, 0)
            turned_residual(1, 0)
            residual(1, 1)
            squares(1, 1)
            turned_residual(1, 1)
            residual_norm(1)
            choose(0)
            choose(1)
            def pick_biases(e):
                for m in range(2):
                    dve.tensor_copy(pick_bias[:, m, :], ident[:, bass.ds(e + E * m, 1)].broadcast_to([P, SLOTS]))

            dve.wait_ge(chosen_ready, 2)
            step(dve.tensor_scalar(pos, chosen, FAR, -FAR, ALU.mult, ALU.add))
            pick_biases(0)
            dve.wait_ge(pos_done, 1)
            step(dve.tensor_tensor(pos, pos, ps[:, X, 0:2 * E].rearrange("p (b e) -> p b e", e=E), ALU.add))

            gain = cols[:, 24:32].rearrange("p (h j a) -> p j h a", h=2, a=1).broadcast_to([P, 4, 2, SLOTS])
            rstd_b = stat[:, 14:16].rearrange("p (b a) -> p b a", a=1).broadcast_to([P, NB, SLOTS])
            iota_b = iota.rearrange("p (a c) -> p a c", a=1).broadcast_to([P, NB, SLOTS])

            def at_expert(tab_ap, e):
                return tab_ap[:, :, bass.ds(e, 1)].broadcast_to([P, NB, SLOTS])

            def select(n, e, slot_ids=iota_b):
                dve.tensor_tensor(sel, slot_ids, at_expert(pos, e), ALU.is_equal).then_inc(sel_step, 1)
                dve.wait_ge(sel_step, n + 1)
                dve.tensor_tensor(sel, sel, rstd_b, ALU.mult).then_inc(sel_ready, 1)

            def select_p(steps, side, e, slot_ids=iota_b):
                half = sel_p[:, :, SLOTS * side:SLOTS * side + SLOTS]
                dve.tensor_tensor(half, slot_ids, at_expert(pos, e), ALU.is_equal).then_inc(selp_step, 1)
                dve.wait_ge(selp_step, steps)
                return dve.tensor_tensor(half, half, at_expert(prob, e), ALU.mult)

            def select_pair(i):
                for side in range(2):
                    ins = select_p(i * 2 + (side + 1), side, i * 2 + side)
                ins.then_inc(selp_ready, 1)

            def gathered_out(n):
                dve.wait_ge(xg_turned, n + 1)
                dve.tensor_tensor(x_g.rearrange("p (h j) c -> p j h c", h=2),
                                  ps[:, X, :].rearrange("p (j h c) -> p j h c", h=2, c=SLOTS),
                                  gain, ALU.mult).then_inc(xg_ready, 1)

            def gate_part(n):
                dve.wait_ge(pieces_used, n * PIECES + 4)
                dve.tensor_scalar(g_act, ps[:, G, :], LIMIT, None, ALU.min).then_inc(g_ready, 1)
                dve.wait_ge(sig_done, n + 1)
                dve.tensor_tensor(g_act, g_act, sig, ALU.mult).then_inc(g_step, 1)

            def up_part(n):
                dve.wait_ge(pieces_used, n * PIECES + 8)
                dve.tensor_scalar(u_act, ps[:, U, :], LIMIT, -LIMIT, ALU.min, ALU.max).then_inc(u_step, 1)
                dve.wait_ge(u_step, n + 1)
                dve.wait_ge(g_step, n + 1)
                dve.scalar_tensor_tensor(a_rows, u_act, 1.0, g_act, ALU.add, ALU.mult).then_inc(act_ready, 1)

            select(0, 0)
            weigh(0)
            weigh(1)
            dve.wait_ge(count_done, 1)
            cnt = ps[0:E, G, 0:1]
            step(dve.tensor_scalar(tab[:, 33:34], cnt, float(SLOTS), None, ALU.is_gt))
            step(dve.tensor_scalar(tab[:, 34:35], cnt, float(2 * SLOTS), None, ALU.is_gt))
            step(dve.tensor_scalar(tab[:, 35:36], cnt, float(3 * SLOTS), None, ALU.is_gt))
            dve.tensor_reduce(tab[:, 32:33], tab[:, 33:36], AX.X, ALU.add).then_inc(nov_ready, 1)
            dve.wait_ge(nov_ready, 1)
            gathered_out(0)
            dve.wait_ge(ostart_done, 1)
            step(dve.tensor_scalar(tab[:, 36:52], iota[0:E, 0:16], ps[0:E, DN, 0:1], None, ALU.subtract))
            step(dve.tensor_scalar(tab[:, 0:16], tab[:, 36:52], tab[:, 32:33], None, ALU.is_lt))
            step(dve.tensor_scalar(tab[:, 16:32], tab[:, 36:52], 0.0, None, ALU.is_ge))
            step(dve.tensor_tensor(tab[:, 16:32], tab[:, 0:16], tab[:, 16:32], ALU.mult))
            step(dve.tensor_scalar(tab[:, 36:52], tab[:, 36:52], 1.0, float(SLOTS), ALU.add, ALU.mult))
            step(dve.tensor_tensor(tab[:, 0:16], tab[:, 36:52], tab[:, 16:32], ALU.mult))
            dve.tensor_scalar(tab[:, 16:32], tab[:, 16:32], cst[0:E, C_EID:C_EID + 1], None, ALU.mult).then_inc(tab_ready, 1)

            def overflow_out():
                dve.wait_ge(tab_done, 1)
                step(dve.tensor_copy(offs, ps[:, DN, 0:16]))
                dve.tensor_copy(over_i[0:1, 0:17], ps[0:1, DN, 16:33]).then_inc(over_ready, 1)

            def pair(i, first=False, last=False):
                for side in range(2):
                    n = i * 2 + side
                    gate_part(n)
                    dve.wait_ge(pieces_used, n * PIECES + 5)
                    if not (last and side):
                        pick_biases(n + 1)
                        select(n + 1, n + 1)
                    if side == 0 and not first:
                        select_pair(i - 1)
                    if last and side:
                        dve.wait_ge(sel_turned, E // 2 - 1)
                        select_pair(E // 2 - 1)
                    up_part(n)
                    if side == 0 and first:
                        overflow_out()
                    if not (last and side):
                        gathered_out(n + 1)

            pair(0, first=True)
            with dve.Fori(1, E // 2 - 1) as i:
                pair(i)
            pair(E // 2 - 1, last=True)

            count = dve.value_load(over_i[0:1, 16:17], min_val=0, max_val=MAX_OVER)
            with dve.If(count > 0):
                with dve.Fori(0, count) as k:
                    n = k + E
                    e = dve.value_load(over_i[0:1, bass.ds(k, 1)], min_val=0, max_val=E - 1)
                    dve.wait_ge(sel_turned, k + E // 2)
                    dve.tensor_tensor(iota_o, iota, offs[:, bass.ds(k, 1)].broadcast_to([P, SLOTS]), ALU.add)\
                       .then_inc(fin_step, 1)
                    dve.wait_ge(fin_step, k + 1)
                    ids = iota_o.rearrange("p (a c) -> p a c", a=1).broadcast_to([P, NB, SLOTS])
                    pick_biases(e)
                    select(n, e, ids)
                    select_p(n + 1, 0, e, ids).then_inc(selp_ready, 1)
                    gathered_out(n)
                    gate_part(n)
                    up_part(n)

            for n in range(2 * NB):
                b, h = divmod(n, 2)
                half = xs[:, b, 512 * h:512 * h + 512]
                dve.wait_ge(combined, (count + E // 2) * 4 - (2 * NB - 1 - n))
                dve.tensor_tensor(half, half, ps[:, Y + n, :], ALU.add).then_inc(res_ready, 1)
            dve.wait_ge(ld_gfin, 16)
            for b in range(NB):
                dve.wait_ge(sq_act, 1 + 2 * (b + 1))
                dve.tensor_tensor(stat[:, 4 + b:5 + b], stat[:, 50 + 2 * b:51 + 2 * b], stat[:, 51 + 2 * b:52 + 2 * b], ALU.add)\
                   .then_inc(fin_sum, 1)
                dve.wait_ge(fin_sum, b + 1)
                variance(2 * NB + b)
                dve.wait_ge(rstd_ready, 2 * NB + b + 1)
                for h in range(2):
                    q = slice(512 * h, 512 * h + 512)
                    dve.scalar_tensor_tensor(xn[:, b, q], xs[:, b, q], stat[:, 16 + b:17 + b], g_fin[:, q], ALU.mult, ALU.mult)\
                       .then_inc(fin_ready, 1)


_INS = ["x", "ln_mix_g", "w_in", "b_gate_a", "b_gate_b", "w_o_a", "w_o_b", "w_out", "ln_ffn_g", "w_router", "b_router",
        "w_gate", "b_gate", "w_up", "b_up", "w_down", "b_down", "ln_final_g"]


def kernel(**inputs):
    import numpy as _np
    import concourse.bacc as _bacc
    from concourse import mybir as _mybir
    from concourse.bass_utils import run_bass_kernel_spmd as _run

    nc = _bacc.Bacc("TRN2", target_bir_lowering=False, num_devices=1)
    arrays, args = {}, []
    given = {name: _np.ascontiguousarray(inputs[name]) for name in _INS}
    given["consts"], given["masks"] = shape_constants()
    for name, a in given.items():
        arrays[f"in_{name}_dram"] = a
        args.append(nc.dram_tensor(f"in_{name}_dram", a.shape, _mybir.dt.from_np(a.dtype), kind="ExternalInput").ap())
    out = nc.dram_tensor("out_dram", (1, SEQ, D), _mybir.dt.float32, kind="ExternalOutput").ap()
    layer(nc, *args, out)
    r = _run(nc, [arrays], core_ids=[0])
    return r.results[0]["out_dram"]
```
